# Optimizing a Trainium2 kernel written in Bass

```python
import jax, jax.numpy as jnp
from jax import lax
import numpy as np

D_MODEL = 1024
BATCH = 1
SEQ = 256
DEPTH = 2

HEAD_DIM = 64
D_MIX = D_MODEL
D_FF = 2752
EPS = 1e-6
NEG_INF = -1e30
BLOCK = 128
CONV_CH = D_MODEL // 2
CONV_WIDTH = 31
SWA_Q_HEADS = (D_MIX - CONV_CH) // HEAD_DIM
SWA_KV_HEADS = 2
SWA_GROUP = SWA_Q_HEADS // SWA_KV_HEADS
SWA_WINDOW = 128
EVEN_IN = 2 * CONV_CH + (SWA_Q_HEADS + 2 * SWA_KV_HEADS) * HEAD_DIM
DIL_HEADS = 8
DIL_PAIRS = ((128, 1), (512, 4), (2048, 16))
POOL_CH = D_MIX - DIL_HEADS * HEAD_DIM
POOL_SIZES = (2, 4, 8, 16)
POOL_GROUP = POOL_CH // len(POOL_SIZES)
ODD_IN = 3 * DIL_HEADS * HEAD_DIM + POOL_CH
N_EVEN = (DEPTH + 1) // 2
N_ODD = DEPTH // 2


def rms_norm(x, g):
    xf = x.astype(jnp.float32)
    y = xf * lax.rsqrt(jnp.mean(xf * xf, axis=-1, keepdims=True) + EPS)
    return (y * g.astype(jnp.float32)).astype(x.dtype)

def layer_norm(x, g, b):
    xf = x.astype(jnp.float32)
    mu = jnp.mean(xf, axis=-1, keepdims=True)
    var = jnp.mean(jnp.square(xf - mu), axis=-1, keepdims=True)
    y = (xf - mu) * lax.rsqrt(var + EPS)
    return (y * g.astype(jnp.float32) + b.astype(jnp.float32)).astype(x.dtype)

def swiglu(x, w_gate, w_up, w_down):
    return (jax.nn.silu(x @ w_gate) * (x @ w_up)) @ w_down

def banded_attention(q, k, v, max_dist, sink=None):
    b, L, kvh, grp, dh = q.shape
    n = -(-L // BLOCK)
    pad = n * BLOCK - L
    qb = jnp.pad(q, ((0, 0), (0, pad), (0, 0), (0, 0), (0, 0))).reshape(b, n, BLOCK, kvh, grp, dh)

    def windows(t):
        tb = jnp.pad(t, ((0, 0), (BLOCK, pad), (0, 0), (0, 0))).reshape(b, n + 1, BLOCK, kvh, dh)
        return jnp.concatenate([tb[:, :-1], tb[:, 1:]], axis=2)

    kw, vw = windows(k), windows(v)
    s = jnp.einsum('bnqhgd,bnkhd->bnhgqk', qb, kw).astype(jnp.float32) * (dh ** -0.5)
    qi = np.arange(BLOCK)[:, None]
    kj = np.arange(2 * BLOCK)[None, :]
    blk = np.arange(n)[:, None, None]
    dist = qi + BLOCK - kj
    valid = (dist >= 0) & (dist <= max_dist) & (blk * BLOCK - BLOCK + kj >= 0)
    s = jnp.where(valid[None, :, None, None], s, NEG_INF)
    m = jnp.max(s, axis=-1)
    if sink is not None:
        m = jnp.maximum(m, sink[None, None, :, :, None])
    p = jnp.exp(s - m[..., None])
    l = jnp.sum(p, axis=-1)
    if sink is not None:
        l = l + jnp.exp(sink[None, None, :, :, None] - m)
    o = jnp.einsum('bnhgqk,bnkhd->bnqhgd', p.astype(v.dtype), vw).astype(jnp.float32)
    m = jnp.moveaxis(m, -1, 2)
    l = jnp.moveaxis(l, -1, 2)
    o = o / l[..., None]

    def to_seq(t):
        return t.reshape(b, n * BLOCK, *t.shape[3:])[:, :L]

    return to_seq(o).astype(q.dtype), to_seq(m), to_seq(l)

def even_mixer(h, w_in, w_out, conv_w, conv_b, ln_g, ln_b, q_g, k_g, sinks):
    b, s, _ = h.shape
    proj = h @ w_in
    cuts = [CONV_CH, 2 * CONV_CH, 2 * CONV_CH + SWA_Q_HEADS * HEAD_DIM,
            2 * CONV_CH + (SWA_Q_HEADS + SWA_KV_HEADS) * HEAD_DIM]
    a_val, a_gate, q, k, v = jnp.split(proj, cuts, axis=-1)
    u = a_val * jax.nn.sigmoid(a_gate)
    u = lax.conv_general_dilated(u, conv_w[:, None, :].astype(u.dtype), (1,), ((CONV_WIDTH - 1, 0),),
                                 dimension_numbers=('NWC', 'WIO', 'NWC'),
                                 feature_group_count=CONV_CH) + conv_b
    u = jax.nn.silu(layer_norm(u, ln_g, ln_b))
    q = rms_norm(q.reshape(b, s, SWA_KV_HEADS, SWA_GROUP, HEAD_DIM), q_g)
    k = rms_norm(k.reshape(b, s, SWA_KV_HEADS, HEAD_DIM), k_g)
    v = v.reshape(b, s, SWA_KV_HEADS, HEAD_DIM)
    o, _, _ = banded_attention(q, k, v, SWA_WINDOW - 1,
                               sinks.reshape(SWA_KV_HEADS, SWA_GROUP).astype(jnp.float32))
    return jnp.concatenate([u, o.reshape(b, s, -1)], axis=-1) @ w_out

def dilated_branch(q, k, v, window, dilation):
    b, s, h, dh = q.shape
    L = s // dilation

    def to_res(t):
        return t.reshape(b, L, dilation, h, dh).transpose(0, 2, 1, 3, 4).reshape(b * dilation, L, h, dh)

    def from_res(t):
        rest = t.shape[2:]
        return t.reshape(b, dilation, L, *rest).swapaxes(1, 2).reshape(b, s, *rest)

    o, m, l = banded_attention(to_res(q)[:, :, :, None], to_res(k), to_res(v), window // dilation)
    return from_res(o[:, :, :, 0]), from_res(m[..., 0]), from_res(l[..., 0])

def multiscale_pool(u, pool_w, pool_scale):
    b, s, _ = u.shape
    uf = u.astype(jnp.float32)
    cs = jnp.pad(jnp.cumsum(uf, axis=1), ((0, 0), (1, 0), (0, 0)))
    outs = []
    for gi, w in enumerate(POOL_SIZES):
        sl = slice(gi * POOL_GROUP, (gi + 1) * POOL_GROUP)
        c = cs[:, :, sl]
        lagged = jnp.pad(c[:, :s + 1 - w], ((0, 0), (w - 1, 0), (0, 0)))
        count = jnp.minimum(jnp.arange(1, s + 1), w).astype(jnp.float32)[:, None]
        pooled = ((c[:, 1:] - lagged) / count - uf[:, :, sl]).astype(u.dtype)
        outs.append(pooled @ pool_w[gi])
    return jnp.concatenate(outs, axis=-1) * pool_scale

def odd_mixer(h, w_in, w_out, q_g, k_g, pool_w, pool_scale):
    b, s, _ = h.shape
    hd = DIL_HEADS * HEAD_DIM
    q, k, v, u = jnp.split(h @ w_in, [hd, 2 * hd, 3 * hd], axis=-1)
    q = rms_norm(q.reshape(b, s, DIL_HEADS, HEAD_DIM), q_g)
    k = rms_norm(k.reshape(b, s, DIL_HEADS, HEAD_DIM), k_g)
    v = v.reshape(b, s, DIL_HEADS, HEAD_DIM)
    outs, ms, ls = zip(*[dilated_branch(q, k, v, w, d) for w, d in DIL_PAIRS])
    ms = jnp.stack(ms)
    wts = jnp.stack(ls) * jnp.exp(ms - jnp.max(ms, axis=0))
    att = jnp.einsum('rbsh,rbshd->bshd', wts, jnp.stack(outs).astype(jnp.float32))
    att = (att / jnp.sum(wts, axis=0)[..., None]).astype(h.dtype)
    pool = multiscale_pool(u, pool_w, pool_scale)
    return jnp.concatenate([att.reshape(b, s, hd), pool], axis=-1) @ w_out

def first_inputs(seed: int = 0) -> dict:
    key = jax.random.key(seed)
    ks = jax.random.split(key, 24)

    def nrm(k, shape, scale):
        return scale * jax.random.normal(k, shape, jnp.float32)

    return {
        "x": nrm(ks[0], (BATCH, SEQ, D_MODEL), 1.0),
        "norm_g": 1.0 + nrm(ks[1], (DEPTH, 3, D_MODEL), 0.05),
        "ffn_w_gate": nrm(ks[2], (DEPTH, 2, D_MODEL, D_FF), D_MODEL ** -0.5),
        "ffn_w_up": nrm(ks[3], (DEPTH, 2, D_MODEL, D_FF), D_MODEL ** -0.5),
        "ffn_w_down": nrm(ks[4], (DEPTH, 2, D_FF, D_MODEL), D_FF ** -0.5),
        "ev_w_in": nrm(ks[5], (N_EVEN, D_MODEL, EVEN_IN), D_MODEL ** -0.5),
        "ev_w_out": nrm(ks[6], (N_EVEN, D_MIX, D_MODEL), D_MIX ** -0.5),
        "ev_conv_w": nrm(ks[7], (N_EVEN, CONV_WIDTH, CONV_CH), CONV_WIDTH ** -0.5),
        "ev_conv_b": nrm(ks[8], (N_EVEN, CONV_CH), 0.02),
        "ev_ln_g": 1.0 + nrm(ks[9], (N_EVEN, CONV_CH), 0.05),
        "ev_ln_b": nrm(ks[10], (N_EVEN, CONV_CH), 0.02),
        "ev_q_norm_g": 1.0 + nrm(ks[11], (N_EVEN, HEAD_DIM), 0.05),
        "ev_k_norm_g": 1.0 + nrm(ks[12], (N_EVEN, HEAD_DIM), 0.05),
        "ev_sinks": nrm(ks[13], (N_EVEN, SWA_Q_HEADS), 0.5),
        "od_w_in": nrm(ks[14], (N_ODD, D_MODEL, ODD_IN), D_MODEL ** -0.5),
        "od_w_out": nrm(ks[15], (N_ODD, D_MIX, D_MODEL), D_MIX ** -0.5),
        "od_q_norm_g": 1.0 + nrm(ks[16], (N_ODD, HEAD_DIM), 0.05),
        "od_k_norm_g": 1.0 + nrm(ks[17], (N_ODD, HEAD_DIM), 0.05),
        "od_pool_w": nrm(ks[18], (N_ODD, len(POOL_SIZES), POOL_GROUP, POOL_GROUP), POOL_GROUP ** -0.5),
        "od_pool_scale": 1.0 + nrm(ks[19], (N_ODD, POOL_CH), 0.05),
    }

def first_block(x, norm_g, ffn_w_gate, ffn_w_up, ffn_w_down,
              ev_w_in, ev_w_out, ev_conv_w, ev_conv_b, ev_ln_g, ev_ln_b,
              ev_q_norm_g, ev_k_norm_g, ev_sinks,
              od_w_in, od_w_out, od_q_norm_g, od_k_norm_g, od_pool_w, od_pool_scale):
    for layer in range(DEPTH):
        g = norm_g[layer]
        x = x + 0.5 * swiglu(rms_norm(x, g[0]), ffn_w_gate[layer, 0], ffn_w_up[layer, 0], ffn_w_down[layer, 0])
        h = rms_norm(x, g[1])
        i = layer // 2
        if layer % 2 == 0:
            mix = even_mixer(h, ev_w_in[i], ev_w_out[i], ev_conv_w[i], ev_conv_b[i], ev_ln_g[i], ev_ln_b[i],
                             ev_q_norm_g[i], ev_k_norm_g[i], ev_sinks[i])
        else:
            mix = odd_mixer(h, od_w_in[i], od_w_out[i], od_q_norm_g[i], od_k_norm_g[i],
                            od_pool_w[i], od_pool_scale[i])
        x = x + mix
        x = x + 0.5 * swiglu(rms_norm(x, g[2]), ffn_w_gate[layer, 1], ffn_w_up[layer, 1], ffn_w_down[layer, 1])
    return x


MLA_HEADS = 4
MLA_Q_RANK = 256
MLA_KV_RANK = 128
MLA_NOPE = 64
MLA_ROPE = 32
MLA_V = 64
ROPE_THETA = 10000.0
CONV_WIDTH_2 = 256
CONV_K = 3
DSA_HEADS = 4
DSA_HEAD_DIM = 64
IDX_HEADS = 8
IDX_DIM = 32
DSA_TOPK_MAX = 256
GLA_HEADS = 4
GLA_DK = 32
GLA_DV = 64
GLA_GATE_RANK = 16
GLA_TAU = 16.0
GLA_CHUNK = 64
N_BRANCH = 4
BRANCH_WIDTH = 256
D_FF_2 = ((8 * D_MODEL + 3 * 256 - 1) // (3 * 256)) * 256
Q_BLOCK = 128
NEG = -1e30

IN_SIZES = (
    MLA_Q_RANK, MLA_KV_RANK, MLA_ROPE,
    CONV_WIDTH_2, CONV_WIDTH_2, CONV_WIDTH_2,
    DSA_HEADS * DSA_HEAD_DIM, DSA_HEAD_DIM, DSA_HEAD_DIM,
    IDX_HEADS * IDX_DIM, IDX_DIM, IDX_HEADS,
    GLA_HEADS * GLA_DK, GLA_HEADS * GLA_DK, GLA_HEADS * GLA_DV,
    GLA_GATE_RANK, GLA_HEADS * GLA_DV,
    N_BRANCH * D_MODEL,
)
IN_TOTAL = sum(IN_SIZES)


def rmsnorm(x, g):
    x32 = x.astype(jnp.float32)
    y = x32 * lax.rsqrt(jnp.mean(x32 * x32, axis=-1, keepdims=True) + EPS)
    return (y * g.astype(jnp.float32)).astype(x.dtype)

def apply_rope(x, positions):
    half = x.shape[-1] // 2
    inv_freq = ROPE_THETA ** (-jnp.arange(half, dtype=jnp.float32) / half)
    ang = positions.astype(jnp.float32)[:, :, None, None] * inv_freq
    cos, sin = jnp.cos(ang), jnp.sin(ang)
    x32 = x.astype(jnp.float32)
    x1, x2 = x32[..., :half], x32[..., half:]
    return jnp.concatenate([x1 * cos - x2 * sin, x1 * sin + x2 * cos], axis=-1).astype(x.dtype)

def to_blocks(a):
    b, s = a.shape[:2]
    return jnp.moveaxis(a.reshape((b, s // Q_BLOCK, Q_BLOCK) + a.shape[2:]), 1, 0)

def from_blocks(a):
    nb, b, qb = a.shape[:3]
    return jnp.moveaxis(a, 0, 1).reshape((b, nb * qb) + a.shape[3:])

def causal_block_attention(q, k, v, scale):
    s_len = k.shape[1]
    key_pos = jnp.arange(s_len)

    def one_block(args):
        qb, start = args
        qpos = start + jnp.arange(Q_BLOCK)
        s = jnp.einsum('bqhd,bkhd->bhqk', qb, k).astype(jnp.float32) * scale
        s = jnp.where(key_pos[None, :] <= qpos[:, None], s, NEG)
        p = jax.nn.softmax(s, axis=-1).astype(v.dtype)
        return jnp.einsum('bhqk,bkhd->bqhd', p, v)

    o = lax.map(one_block, (to_blocks(q), jnp.arange(s_len // Q_BLOCK) * Q_BLOCK))
    return from_blocks(o)

def mla_branch(cq, ckv, krope, positions, q_norm_g, w_q_up, kv_norm_g, w_kv_up):
    b, s, _ = cq.shape
    q = (rmsnorm(cq, q_norm_g) @ w_q_up).reshape(b, s, MLA_HEADS, MLA_NOPE + MLA_ROPE)
    q = jnp.concatenate([q[..., :MLA_NOPE], apply_rope(q[..., MLA_NOPE:], positions)], axis=-1)
    kv = (rmsnorm(ckv, kv_norm_g) @ w_kv_up).reshape(b, s, MLA_HEADS, MLA_NOPE + MLA_V)
    k_rope = apply_rope(krope[:, :, None, :], positions)
    k = jnp.concatenate([kv[..., :MLA_NOPE], jnp.broadcast_to(k_rope, (b, s, MLA_HEADS, MLA_ROPE))], axis=-1)
    v = kv[..., MLA_NOPE:]
    o = causal_block_attention(q, k, v, (MLA_NOPE + MLA_ROPE) ** -0.5)
    return o.reshape(b, s, MLA_HEADS * MLA_V)

def shortconv_branch(cb, cc, cx, conv_w):
    u = cc * cx
    y = lax.conv_general_dilated(
        u, conv_w[:, None, :], window_strides=(1,), padding=[(CONV_K - 1, 0)],
        dimension_numbers=('NWC', 'WIO', 'NWC'), feature_group_count=CONV_WIDTH_2)
    return cb * y

def dsa_branch(dq, dk, dv, iq, ik, iw):
    b, s, _ = dq.shape
    topk = min(DSA_TOPK_MAX, s // 4)
    q = dq.reshape(b, s, DSA_HEADS, DSA_HEAD_DIM)
    q_idx = iq.reshape(b, s, IDX_HEADS, IDX_DIM)
    key_pos = jnp.arange(s)
    gather = jax.vmap(lambda a, i: a[i])

    def one_block(args):
        qb, qib, wb, start = args
        qpos = start + jnp.arange(Q_BLOCK)
        rel = jax.nn.relu(jnp.einsum('bqhd,bsd->bqhs', qib, ik).astype(jnp.float32) * IDX_DIM ** -0.5)
        score = jnp.einsum('bqh,bqhs->bqs', wb.astype(jnp.float32) * IDX_HEADS ** -0.5, rel)
        score = jnp.where(key_pos[None, None, :] <= qpos[None, :, None], score, NEG)
        _, idx = lax.top_k(score, topk)
        valid = idx <= qpos[None, :, None]
        k_sel = gather(dk, idx)
        v_sel = gather(dv, idx)
        att = jnp.einsum('bqhd,bqkd->bqhk', qb, k_sel).astype(jnp.float32) * DSA_HEAD_DIM ** -0.5
        att = jnp.where(valid[:, :, None, :], att, NEG)
        p = jax.nn.softmax(att, axis=-1).astype(dv.dtype)
        return jnp.einsum('bqhk,bqkd->bqhd', p, v_sel)

    o = lax.map(one_block, (to_blocks(q), to_blocks(q_idx), to_blocks(iw), jnp.arange(s // Q_BLOCK) * Q_BLOCK))
    return from_blocks(o).reshape(b, s, DSA_HEADS * DSA_HEAD_DIM)

def gla_branch(gq, gk, gv, glr, gr, w_gate_up, b_gate, norm_g):
    b, s, _ = gq.shape
    nc = s // GLA_CHUNK
    f32 = jnp.float32

    def chunks(a, d):
        return a.astype(f32).reshape(b, nc, GLA_CHUNK, GLA_HEADS, d).transpose(1, 0, 3, 2, 4)

    q = chunks(gq, GLA_DK) * GLA_DK ** -0.5
    k = chunks(gk, GLA_DK)
    v = chunks(gv, GLA_DV)
    log_alpha = jax.nn.log_sigmoid((glr @ w_gate_up + b_gate).astype(f32)) / GLA_TAU
    g = chunks(log_alpha, GLA_DK)
    causal = jnp.tril(jnp.ones((GLA_CHUNK, GLA_CHUNK), dtype=bool))

    def step(state, inp):
        qc, kc, vc, gc = inp
        cum = lax.cumsum(gc, axis=2)
        o_inter = jnp.einsum('bhik,bhkv->bhiv', qc * jnp.exp(cum), state)
        decay = jnp.exp(jnp.where(causal[:, :, None], cum[:, :, :, None, :] - cum[:, :, None, :, :], NEG))
        attn = jnp.einsum('bhik,bhjk,bhijk->bhij', qc, kc, decay)
        o_intra = jnp.einsum('bhij,bhjv->bhiv', attn, vc)
        last = cum[:, :, -1:, :]
        state = jnp.exp(last[:, :, 0, :])[..., None] * state + jnp.einsum('bhjk,bhjv->bhkv', kc * jnp.exp(last - cum), vc)
        return state, o_inter + o_intra

    state0 = jnp.zeros((b, GLA_HEADS, GLA_DK, GLA_DV), f32)
    _, o = lax.scan(step, state0, (q, k, v, g))
    o = o.transpose(1, 0, 3, 2, 4).reshape(b, s, GLA_HEADS, GLA_DV)
    o = rmsnorm(o, norm_g).astype(gr.dtype).reshape(b, s, GLA_HEADS * GLA_DV)
    return jax.nn.silu(gr) * o

def second_inputs(seed: int = 0) -> dict:
    key = jax.random.key(seed)
    ks = jax.random.split(key, 20)
    f32 = jnp.float32

    def nrm(k, shape, scale):
        return jax.random.normal(k, shape, f32) * scale

    def gain(k, shape):
        return 1.0 + 0.05 * jax.random.normal(k, shape, f32)

    return {
        'x': nrm(ks[0], (BATCH, SEQ, D_MODEL), 1.0),
        'positions': jnp.broadcast_to(jnp.arange(SEQ, dtype=jnp.int32)[None, :], (BATCH, SEQ)),
        'attn_norm_g': gain(ks[1], (DEPTH, D_MODEL)),
        'w_in': nrm(ks[2], (DEPTH, D_MODEL, IN_TOTAL), D_MODEL ** -0.5),
        'mla_q_norm_g': gain(ks[3], (DEPTH, MLA_Q_RANK)),
        'mla_w_q_up': nrm(ks[4], (DEPTH, MLA_Q_RANK, MLA_HEADS * (MLA_NOPE + MLA_ROPE)), MLA_Q_RANK ** -0.5),
        'mla_kv_norm_g': gain(ks[5], (DEPTH, MLA_KV_RANK)),
        'mla_w_kv_up': nrm(ks[6], (DEPTH, MLA_KV_RANK, MLA_HEADS * (MLA_NOPE + MLA_V)), MLA_KV_RANK ** -0.5),
        'conv_w': nrm(ks[7], (DEPTH, CONV_K, CONV_WIDTH_2), CONV_K ** -0.5),
        'gla_w_gate_up': nrm(ks[8], (DEPTH, GLA_GATE_RANK, GLA_HEADS * GLA_DK), GLA_GATE_RANK ** -0.5),
        'gla_b_gate': nrm(ks[9], (DEPTH, GLA_HEADS * GLA_DK), 0.1),
        'gla_norm_g': gain(ks[10], (DEPTH, GLA_DV)),
        'w_branch': nrm(ks[11], (DEPTH, N_BRANCH, BRANCH_WIDTH, D_MODEL), BRANCH_WIDTH ** -0.5),
        'w_out': nrm(ks[12], (DEPTH, D_MODEL, D_MODEL), D_MODEL ** -0.5),
        'ffn_norm_g': gain(ks[13], (DEPTH, D_MODEL)),
        'w_ffn_gate': nrm(ks[14], (DEPTH, D_MODEL, D_FF_2), D_MODEL ** -0.5),
        'w_ffn_up': nrm(ks[15], (DEPTH, D_MODEL, D_FF_2), D_MODEL ** -0.5),
        'w_ffn_down': nrm(ks[16], (DEPTH, D_FF_2, D_MODEL), D_FF_2 ** -0.5),
        'final_norm_g': gain(ks[17], (D_MODEL,)),
    }

def second_block(x, positions, attn_norm_g, w_in, mla_q_norm_g, mla_w_q_up, mla_kv_norm_g, mla_w_kv_up,
              conv_w, gla_w_gate_up, gla_b_gate, gla_norm_g, w_branch, w_out, ffn_norm_g,
              w_ffn_gate, w_ffn_up, w_ffn_down, final_norm_g):
    b, s, d = x.shape
    split_points = [int(p) for p in np.cumsum(IN_SIZES)[:-1]]
    for l in range(DEPTH):
        h = rmsnorm(x, attn_norm_g[l])
        (cq, ckv, krope, cb, cc, cx, dq, dk, dv, iq, ik, iw,
         gq, gk, gv, glr, gr, gate_pre) = jnp.split(h @ w_in[l], split_points, axis=-1)

        o_mla = mla_branch(cq, ckv, krope, positions, mla_q_norm_g[l], mla_w_q_up[l],
                           mla_kv_norm_g[l], mla_w_kv_up[l])
        o_conv = shortconv_branch(cb, cc, cx, conv_w[l])
        o_dsa = dsa_branch(dq, dk, dv, iq, ik, iw)
        o_gla = gla_branch(gq, gk, gv, glr, gr, gla_w_gate_up[l], gla_b_gate[l], gla_norm_g[l])

        gates = jax.nn.sigmoid(gate_pre).reshape(b, s, N_BRANCH, d)
        branches = (o_mla, o_conv, o_dsa, o_gla)
        merged = gates[:, :, 0, :] * (branches[0] @ w_branch[l, 0])
        for n in range(1, N_BRANCH):
            merged = merged + gates[:, :, n, :] * (branches[n] @ w_branch[l, n])
        x = x + merged @ w_out[l]

        h2 = rmsnorm(x, ffn_norm_g[l])
        x = x + (jax.nn.silu(h2 @ w_ffn_gate[l]) * (h2 @ w_ffn_up[l])) @ w_ffn_down[l]
    return rmsnorm(x, final_norm_g)


def setup_inputs(seed=0):
    out = dict(first_inputs(seed))
    for name, value in second_inputs(seed + 1).items():
        if name != "x":
            out[name + "_2"] = value
    return out


def reference(
    x, norm_g, ffn_w_gate, ffn_w_up, ffn_w_down, ev_w_in, ev_w_out, ev_conv_w, ev_conv_b,
    ev_ln_g, ev_ln_b, ev_q_norm_g, ev_k_norm_g, ev_sinks, od_w_in, od_w_out, od_q_norm_g,
    od_k_norm_g, od_pool_w, od_pool_scale, positions_2, attn_norm_g_2, w_in_2, mla_q_norm_g_2,
    mla_w_q_up_2, mla_kv_norm_g_2, mla_w_kv_up_2, conv_w_2, gla_w_gate_up_2, gla_b_gate_2,
    gla_norm_g_2, w_branch_2, w_out_2, ffn_norm_g_2, w_ffn_gate_2, w_ffn_up_2, w_ffn_down_2,
    final_norm_g_2,
):
    x = first_block(
        x, norm_g, ffn_w_gate, ffn_w_up, ffn_w_down, ev_w_in, ev_w_out, ev_conv_w, ev_conv_b,
        ev_ln_g, ev_ln_b, ev_q_norm_g, ev_k_norm_g, ev_sinks, od_w_in, od_w_out, od_q_norm_g,
        od_k_norm_g, od_pool_w, od_pool_scale,
    )
    return second_block(
        x, positions_2, attn_norm_g_2, w_in_2, mla_q_norm_g_2, mla_w_q_up_2, mla_kv_norm_g_2,
        mla_w_kv_up_2, conv_w_2, gla_w_gate_up_2, gla_b_gate_2, gla_norm_g_2, w_branch_2,
        w_out_2, ffn_norm_g_2, w_ffn_gate_2, w_ffn_up_2, w_ffn_down_2, final_norm_g_2,
    )


_drawn_inputs = setup_inputs


def setup_inputs(seed=0):
    import zlib

    import numpy as np

    out = dict(_drawn_inputs(seed))
    spreads = {}
    factors = {'ev_ln_b': 3.139,
     'ev_q_norm_g': 4.541,
     'ev_k_norm_g': 4.591,
     'ev_sinks': 5.369,
     'od_q_norm_g': 4.733,
     'od_k_norm_g': 5.153,
     'mla_q_norm_g_2': 8.0,
     'mla_kv_norm_g_2': 5.663,
     'gla_b_gate_2': 3.865,
     'gla_norm_g_2': 3.167}
    for name, (base, spread) in spreads.items():
        noise = np.random.default_rng([zlib.crc32(name.encode()), seed]).standard_normal(out[name].shape)
        drawn = base * np.exp(spread * noise) if base else spread * noise
        out[name] = __import__('jax').numpy.asarray(drawn.astype(out[name].dtype))
    for name, factor in factors.items():
        out[name] = (out[name] * factor).astype(out[name].dtype)
    return out
```

```python
from contextlib import ExitStack

import numpy as np
import concourse.bass as bass
from concourse import mybir

F32 = mybir.dt.float32
F32R = mybir.dt.float32r
I32 = mybir.dt.int32
ALU = mybir.AluOpType
ACT = mybir.ActivationFunctionType
AX = mybir.AxisListType.X

D = 1024
KD = 8
S = 256
F1 = 2752
F2 = 2816
EPS = 1e-6
NEG = -1e30
TAKEN = -3e38
CH = 2048
NS = 3
NH = 2
CONV_W = 31
PAD = 32

CONSTS = {}


def _consts():
    parts = []

    def put(name, a):
        a = np.ascontiguousarray(a, dtype=np.float32).reshape(128, -1)
        CONSTS[name] = (sum(p.shape[1] for p in parts), a.shape[1])
        parts.append(a)

    put("ident", np.eye(128))
    put("ones", np.full((128, 128), 1.0 / 512))
    half = 16
    inv = (np.float32(10000.0) ** (-np.arange(half, dtype=np.float32) / np.float32(half))).astype(np.float32)
    put("invf", np.broadcast_to(inv, (128, half)))
    q = np.arange(128)[:, None]
    dist = [q - np.arange(128)[None, :], q + 128 - np.arange(256)[None, :]]

    def both(f):
        return np.concatenate([f(d) for d in dist], axis=1)

    def hide(ok):
        return np.where(ok, 0.0, NEG)

    keep = sum(p.shape[1] for p in parts)
    put("swa", both(lambda d: hide((d >= 0) & (d <= 127))))
    put("dil", both(lambda d: hide((d >= 0) & ((d <= 128) | (d % 4 == 0)))))
    put("mult", both(lambda d: np.where(d >= 0, (d <= 128) * 1.0 + (d % 4 == 0) + (d % 16 == 0), 0.0)))
    rc = np.ones((4, 16))
    for g, w in enumerate((2, 4, 8, 16)):
        rc[g] = 1.0 / np.minimum(np.arange(1, 17), w)
    put("rcount", np.broadcast_to(rc.reshape(1, -1), (128, 64)))
    first = np.concatenate(parts, axis=1)
    del parts[1:]
    parts[0] = first[:, 0:keep]
    put("causal", both(lambda d: hide(d >= 0)))
    j, i = np.arange(128)[:, None], np.arange(128)[None, :]
    lv = [(j == i)]
    for s in (1, 2, 4, 8, 16, 32):
        lv.append((j // (2 * s) == i // (2 * s)) & ((j // s) % 2 == 0) & ((i // s) % 2 == 1))
    put("levels", np.concatenate(lv, axis=1))
    put("block", (j // 32 == np.arange(256)[None, :] // 64))
    second = np.concatenate(parts, axis=1)[:, keep:]
    out = np.zeros((128, first.shape[1] + second.shape[1]), np.float32)
    out[:, 0:first.shape[1]] = first
    out[:, first.shape[1]:] = second
    return out, keep, first.shape[1], second.shape[1]


CONST_ARRAY, KEEP, FIRST, SECOND = _consts()


class Queues:

    def __init__(self, nc, ctx):
        self.nc, self.ctx = nc, ctx
        self.q = {e: [] for e in ("pe", "act", "dve", "pool", "sp")}
        self.sem = {e: ctx.enter_context(nc.semaphore("s_" + e)) for e in ("pe", "act", "dve", "pool")}
        self.n = dict.fromkeys(self.q, 0)
        self.seen = {e: {} for e in self.q}
        self.names = {}
        self.pend = {e: [] for e in self.q}

    def waits(self, e, after):
        for a in after:
            if a is None:
                continue
            if isinstance(a, list):
                self.waits(e, a)
                continue
            s, v = a
            if self.seen[e].get(id(s), 0) < v:
                self.seen[e][id(s)] = v
                self.q[e].append(("wait", s, v))

    def op(self, e, fn, *after, sig=True):
        if self.pend[e]:
            p, self.pend[e] = self.pend[e], []
            self.waits(e, p)
        self.waits(e, after)
        if not sig:
            self.q[e].append(("op", fn, None, 0))
            return None
        self.n[e] += 1
        self.q[e].append(("op", fn, self.sem[e], 1))
        return (self.sem[e], self.n[e])

    def dma(self, e, out, src, sem, value, *after, **k):
        self.waits(e, after)
        self.q[e].append(("op", lambda g, o=out, s=src, k=k: g.dma_start(o, s, **k), sem, 16))
        return (sem, value)

    def last(self, e):
        return (self.sem[e], self.n[e]) if self.n[e] else None

    def fence(self, *more):
        t = [self.last(e) for e in ("pe", "act", "dve", "pool")] + list(more)
        for e in ("pe", "act", "dve", "pool"):
            self.pend[e] = [x for x in t if x is not None]

    def emit(self, block):
        for e, deco in (("pe", block.tensor), ("act", block.scalar), ("dve", block.vector),
                        ("pool", block.gpsimd), ("sp", block.sync)):
            items = self.q[e]

            def run(eng, items=items):
                for it in items:
                    if it[0] == "wait":
                        eng.wait_ge(it[1], it[2])
                    else:
                        ins = it[1](eng)
                        if it[2] is not None:
                            ins.then_inc(it[2], it[3])
            deco(run)


def build(nc, A, out, upto=99, frm=0):
    ctx = ExitStack()
    with ctx:
        Q = Queues(nc, ctx)
        op = Q.op

        def sb(name, shape, dt=F32, c=ctx):
            return c.enter_context(nc.sbuf_tensor(name, shape, dt))

        class Region:

            def __init__(self, t, lo, hi):
                self.t, self.at, self.hi = t, lo, hi

            def __call__(self, name, shape, c=None):
                n = int(np.prod(shape[1:]))
                v = self.t[0:shape[0], self.at:self.at + n]
                self.at += n
                assert self.at <= self.hi, (name, self.at, self.hi)
                if len(shape) == 3:
                    v = v.rearrange("p (a b) -> p a b", a=shape[1])
                if len(shape) == 4:
                    v = v.rearrange("p (a b c) -> p a b c", a=shape[1], b=shape[2])
                return v

        def sem(name):
            return ctx.enter_context(nc.semaphore(name))

        PS = ctx.enter_context(nc.psum_tensor("ps", [128, 8, 512], F32))
        banks = [PS[:, i, :] for i in range(8)]
        free = [(i, None) for i in range(8)]

        def bank():
            i, t = free.pop(0)
            return i, banks[i], t

        def pair(bb):
            i = bb[0][0]
            return PS[:, i:i + 2, :]

        def bank2():
            at = {i: n for n, (i, _) in enumerate(free)}
            i = min((i for i in at if i % 2 == 0 and i + 1 in at), key=lambda i: max(at[i], at[i + 1]))
            bb = [free[at[j]] for j in (i, i + 1)]
            for x in bb:
                free.remove(x)
            return [(j, banks[j], t) for j, t in bb]

        def release(i, *t):
            free.append((i, list(t)))

        def mm(o, l, r, start, stop, *after, sig=None):
            return op("pe", lambda e: e.matmul(o, l, r, start=start, stop=stop), *after,
                      sig=stop if sig is None else sig)

        def mm3(o, lh, ll, rh, rl, start, stop, *after, sig=False):
            mm(o, lh, rh, start, False, *after, sig=False)
            mm(o, lh, rl, False, False, sig=False)
            return mm(o, ll, rh, False, stop, sig=sig)

        def tp(o, i, idn, *after, sig=True):
            return op("pe", lambda e: e.transpose(o, i, idn), *after, sig=sig)

        def act(o, i, f, *after, **k):
            return op("act", lambda e: e.activation(o, i, f, **k), *after)

        def cp(o, i, *after, e="dve"):
            if e == "act":
                return act(o, i, ACT.Copy, *after)
            return op(e, lambda g: g.tensor_copy(o, i), *after)

        def tt(o, a, b, f, *after, e="dve"):
            return op(e, lambda g: g.tensor_tensor(o, a, b, f), *after)

        def ts(o, a, s1, s2, f1, f2, *after, e="dve"):
            if f2 is None:
                return op(e, lambda g: g.tensor_scalar(o, a, s1, None, f1), *after)
            return op(e, lambda g: g.tensor_scalar(o, a, s1, s2, f1, f2), *after)

        def stt(o, a, s, b, f1, f2, *after):
            return op("dve", lambda g: g.scalar_tensor_tensor(out=o, in0=a, scalar=s, in1=b, op0=f1, op1=f2), *after)

        def ttr(o, a, b, scale, init, f1, f2, acc, *after):
            return op("dve", lambda g: g.tensor_tensor_reduce(out=o, in0=a, in1=b, scale=scale, scalar=init,
                                                              op0=f1, op1=f2, accum_out=acc), *after)

        def red(o, a, f, *after):
            return op("dve", lambda g: g.tensor_reduce(o, a, AX, f), *after)

        def rcp(o, a, *after):
            return op("dve", lambda g: g.reciprocal(o, a), *after)

        def memset(o, v, *after, e="pool"):
            return op(e, lambda g: g.memset(o, v), *after)

        xs = sb("xs", [128, 2, D])
        hTh = sb("hTh", [128, KD, S], F32R)
        hTl = sb("hTl", [128, KD, S], F32R)
        stage = [sb(f"stage{i}", [128, CH]) for i in range(NS)]
        whi = [sb(f"whi{i}", [128, CH], F32R) for i in range(NH)]
        wlo = [sb(f"wlo{i}", [128, CH], F32R) for i in range(NH)]
        NCC = max(FIRST, KEEP + SECOND)
        cst = sb("cst", [128, NCC])
        st8 = sb("st8", [128, 16])
        phalf = sb("phalf", [128, 32])
        gcol = sb("gcol", [128, 8, 11])
        junk = sb("junk", [128, D], mybir.dt.bfloat16)
        R2 = sb("R2", [128, 2 * S])
        dg = sb("dg", [128, 2, 128])

        def C(name, lo=0, n=None):
            o, w = CONSTS[name]
            return cst[:, o + lo:o + (w if n is None else lo + n)]

        ident = C("ident")
        s_x, s_c, s_o = sem("s_x"), sem("s_c"), sem("s_o")
        s_st = [sem(f"s_st{i}") for i in range(NS)]
        s_g = sem("s_g")
        s_par = sem("s_par")

        s_k = sem("s_k")
        Q.dma("sp", xs[:, :, :], A["x"][0].rearrange("(t p) d -> p t d", p=128), s_x, 16)
        t_c = Q.dma("sp", cst[:, 0:KEEP], A["consts"][:, 0:KEEP], s_k, 16)
        t_x = {(t, n): (s_x, 16) for t in range(2) for n in range(2)}
        t_ph = memset(phalf[:, :], -0.5)
        npar = [0]

        def par(o, src, *after):
            npar[0] += 16
            return Q.dma("act", o, src, s_par, npar[0], *after, allow_slow_non_contiguous=True)

        plan = []

        def view(c, shape):
            n = int(np.prod(shape))
            v = c[:, 0:n]
            if len(shape) == 2:
                return v.rearrange("p (a b) -> p a b", a=shape[0])
            return v

        def plan_cols(w, k0, nk, c0, nc_):
            src = w[k0 * 128:(k0 + nk) * 128, c0:c0 + nc_].rearrange("(k p) n -> p k n", p=128)
            plan.append(([(0, src, (nk, nc_))], nk * nc_))

        def plan_rows(w, rows):
            plan.append(([(i * 1024, w[r:r + 128, :], (1, 1024)) for i, r in enumerate(rows)], 1024 * len(rows)))

        def plan_up(wg, wu, F):
            c = 0
            while c < F:
                n = min(256, F - c)
                plan_cols(wg, 0, 8, c, n)
                plan_cols(wu, 0, 8, c, n)
                c += n

        def row_starts(F):
            r = [i * 128 for i in range(F // 128)]
            if F % 128:
                r.append(F - 128)
            return r

        def plan_down(w, F):
            r = row_starts(F)
            for i in range(0, len(r), 2):
                plan_rows(w, r[i:i + 2])

        def plan_x(w, c0, n):
            if n <= 256:
                plan_cols(w, 0, 8, c0, n)
            else:
                plan_cols(w, 0, 4, c0, n)
                plan_cols(w, 4, 4, c0, n)

        ffns = []
        for l in range(2):
            for s in range(2):
                ffns.append((A["ffn_w_gate"][l, s], A["ffn_w_up"][l, s], A["ffn_w_down"][l, s], F1))
        for l in range(2):
            ffns.append((A["w_ffn_gate_2"][l], A["w_ffn_up_2"][l], A["w_ffn_down_2"][l], F2))

        def plan_ffn(i):
            wg, wu, wd, F = ffns[i]
            plan_up(wg, wu, F)
            plan_down(wd, F)

        ev, od = A["ev_w_in"][0], A["od_w_in"][0]
        X2 = [(0, 416), (1184, 512), (1696, 512), (2208, 440)]

        FILL = [(1, False), (3, False), (1, True), (2, False), (0, False), (3, True), (2, True), (0, True)]

        def plan_even():
            for c in (0, 256):
                plan_cols(ev, 0, 8, c, 256)
                plan_cols(ev, 0, 8, 512 + c, 256)
            plan_x(ev, 1024, 512)
            plan_x(ev, 1536, 256)
            plan_down(A["ev_w_out"][0], 1024)

        def plan_odd():
            for c in (0, 512, 1024):
                plan_x(od, c, 512)
            for c in (1536, 1792):
                plan_cols(od, 0, 8, c, 256)
            plan_down(A["od_w_out"][0], 1024)

        def plan_mixer2(l):
            w2 = A["w_in_2"][l]
            for c, n in X2:
                plan_x(w2, c, n)
            for c in (416, 672, 928):
                plan_cols(w2, 0, 8, c, 256)
            for n, merge in FILL:
                if merge:
                    plan_rows(A["w_branch_2"][l, n], [0, 128])
                else:
                    for c in range(4):
                        plan_cols(w2, 0, 8, 2648 + 1024 * n + 256 * c, 256)
            plan_down(A["w_out_2"][l], 1024)

        plans = [lambda: plan_ffn(0), plan_even, lambda: plan_ffn(1), lambda: plan_ffn(2), plan_odd,
                 lambda: plan_ffn(3), lambda: plan_mixer2(0), lambda: plan_ffn(4), lambda: plan_mixer2(1),
                 lambda: plan_ffn(5)]
        for p in plans[frm:upto]:
            p()

        stage_free = [None] * NS
        stage_ready = {}
        half_free = [None] * NH
        split_done = {}
        nxt = {"dma": 0, "split": 0, "use": 0}

        def issue_dma():
            i = nxt["dma"]
            if i >= len(plan):
                return
            nxt["dma"] += 1
            s = i % NS
            parts, n = plan[i]
            k = stage_count[s]
            for off, src, shape in parts:
                k += 1
                dst = stage[s][:, off:off + shape[0] * shape[1]]
                if len(src.shape) == 3:
                    dst = dst.rearrange("p (a b) -> p a b", a=shape[0])
                t = Q.dma("sp", dst, src, s_st[s], 16 * k, stage_free[s])
            stage_count[s] = k
            stage_ready[i] = t

        stage_count = [0] * NS

        def issue_split():
            i = nxt["split"]
            if i >= len(plan):
                return
            nxt["split"] += 1
            s, h = i % NS, i % NH
            n = plan[i][1]
            for a, b in ((0, n // 2), (n // 2, n)):
                t1 = act(whi[h][:, a:b], stage[s][:, a:b], ACT.Copy, stage_ready[i], half_free[h])
                t2 = tt(wlo[h][:, a:b], stage[s][:, a:b], whi[h][:, a:b].bitcast(F32), ALU.subtract, t1, half_free[h])
            stage_free[s] = t2
            split_done[i] = t2
            issue_dma()

        def take():
            i = nxt["use"]
            nxt["use"] += 1
            return i, whi[i % NH], wlo[i % NH], split_done[i]

        later = []

        def used(i, t):
            half_free[i % NH] = t
            issue_split()
            for g in list(later):
                if next(g, "end") == "end":
                    later.remove(g)

        def flush():
            for g in list(later):
                for _ in g:
                    pass
                later.remove(g)

        issue_dma()
        gsrc = [A["norm_g"][l, j] for l in range(2) for j in range(3)]
        for l in range(2):
            gsrc += [A["attn_norm_g_2"][l], A["ffn_norm_g_2"][l]]
        rope = sb("rope", [128, 2, 2, 16])
        cr = ctx.enter_context(ExitStack())
        grow = sb("grow", [10, D], c=cr)
        for i, g in enumerate(gsrc):
            Q.dma("act", grow[i:i + 1, :], g.rearrange("(a n) -> a n", a=1), s_g, 16 * (i + 1))
        t_g = (s_g, 160)
        issue_dma()
        t_c1 = Q.dma("sp", cst[:, KEEP:FIRST], A["consts"][:, KEEP:FIRST], s_c, 16)
        for _ in range(NS - 2):
            issue_dma()

        def split_T(ps, dh, dl, t, scale=1.0):
            a = act(dh, ps, ACT.Copy, t, scale=scale)
            if scale == 1.0:
                return tt(dl, ps, dh.bitcast(F32), ALU.subtract, a)
            return stt(dl, ps, scale, dh.bitcast(F32), ALU.mult, ALU.subtract, a)

        def transposed(src, nk, dh, dl, after):
            toks = []
            for k0 in range(0, nk, 2):
                b, ps, f = bank()
                m = min(2, nk - k0)
                for j in range(m):
                    for t in range(2):
                        c = (2 * j + t) * 128
                        w = tp(ps[:, c:c + 128], src(k0 + j, t), ident, f, after(k0 + j, t), t_c,
                               sig=(j == m - 1 and t == 1))
                o = slice(k0, k0 + m)
                z = split_T(ps[:, 0:m * 256], dh[:, o, :].rearrange("p k s -> p (k s)"),
                            dl[:, o, :].rearrange("p k s -> p (k s)"), w)
                release(b, z)
                toks.append(z)
            return toks

        def power(o, a, n, *after):
            return tt(o, a, phalf[:, 0:n], ALU.pow, *after, t_ph, e="pool")

        def rms_col(tin):
            a = Q.last("act")
            for t in range(2):
                a = act(junk[:, :], xs[:, t, :], ACT.Square, tin[t, 0], tin[t, 1], a, accum_out=st8[:, t:t + 1])
            b = ts(st8[:, 2:4], st8[:, 0:2], 1.0 / D, EPS, ALU.mult, ALU.add, a)
            return power(st8[:, 4:6], st8[:, 2:4], 2, b)

        def norm_T(i, tin):
            hr = []
            for k in range(KD):
                b, ps, f = bank()
                for t in range(2):
                    w = tp(ps[:, t * 128:t * 128 + 128], xs[:, t, k * 128:k * 128 + 128], ident, f,
                           tin[t, k // 4], t_c, sig=(t == 1))
                g = gcol[:, k, i:i + 1]
                a = act(hTh[:, k, :], ps[:, 0:256], ACT.Copy, w, t_gc, scale=g)
                z = stt(hTl[:, k, :], ps[:, 0:256], g, hTh[:, k, :].bitcast(F32), ALU.mult, ALU.subtract, a)
                release(b, z)
                hr.append(z)
            tcol = rms_col(tin)

            def row():
                for t in range(2):
                    z = ts(dg[:, t, :], ident, st8[:, 4 + t:5 + t], 512.0, ALU.mult, ALU.mult, tcol)
                b, ps, f = bank()
                for t in range(2):
                    w = mm(ps[:, t * 128:t * 128 + 128], C("ones"), dg[:, t, :], True, True, f, z)
                z = cp(R2[:, :].rearrange("p (a s) -> p a s", a=2), ps[:, 0:256].unsqueeze(1).broadcast_to([128, 2, 256]), w)
                release(b, z)
                return z

            return hr, tcol, row

        R22 = R2[:, :].rearrange("p (a s) -> p a s", a=2)
        R24 = R2[:, :].unsqueeze(1).broadcast_to([128, 2, 2 * S])

        def two(x):
            return x.rearrange("p (a s) -> p a s", a=2)

        def up_tile(ps, c0, wh, wl, w_cols, col, sd, hready, f):
            wvh, wvl = view(wh, (8, w_cols)), view(wl, (8, w_cols))
            for k in range(8):
                t = mm3(ps[:, c0:c0 + 256], wvh[:, k, col:col + 128], wvl[:, k, col:col + 128],
                        hTh[:, k, :], hTl[:, k, :], k == 0, k == 7, f, sd, hready[k], sig=(k == 7))
            return t

        def x_cols(n, hready):
            bb = [bank(), bank()]
            nk = 8 if n <= 256 else 4
            for c in range(8 // nk):
                i, wh, wl, sd = take()
                vh, vl = view(wh, (nk, n)), view(wl, (nk, n))
                toks = []
                for t in range(2):
                    sl = slice(t * 128, t * 128 + 128)
                    for kk in range(nk):
                        k = c * nk + kk
                        tk = mm3(bb[t][1][:, 0:n], hTh[:, k, sl], hTl[:, k, sl], vh[:, kk, :], vl[:, kk, :],
                                 k == 0, k == 7, bb[t][2], sd, hready[k], sig=(kk == nk - 1))
                    toks.append(tk)
                used(i, toks[-1])
            return [(bb[t][0], bb[t][1], toks[t]) for t in range(2)]

        def by_token(o, ps, t, *after, e="act"):
            if e == "act":
                return act(o, ps, ACT.Copy, *after, scale=st8[:, 4 + t:5 + t])
            return ts(o, ps, st8[:, 4 + t:5 + t], None, ALU.mult, None, *after)

        def down(parts, coef, xfree=None):
            bb = [[bank() for n in range(2)] for t in range(2)]
            nk = len(parts)
            for k0 in range(0, nk, 2):
                i, wh, wl, sd = take()
                for n in range(2):
                    for t in range(2):
                        for k in range(k0, min(nk, k0 + 2)):
                            h, lo, sl, tk = parts[k]
                            c = (k - k0) * 1024 + n * 512
                            w = mm3(bb[t][n][1][:, :], h[sl, t * 128:t * 128 + 128], lo[sl, t * 128:t * 128 + 128],
                                    wh[sl, c:c + 512], wl[sl, c:c + 512], k == 0, k == nk - 1,
                                    bb[t][n][2], sd, tk, sig=(k == nk - 1 or (t == 1 and n == 1 and k % 2 == 1)))
                        bb[t][n] = (bb[t][n][0], bb[t][n][1], bb[t][n][2], w)
                used(i, w)
            toks = {}
            for n in range(2):
                for t in range(2):
                    b, ps, _, w = bb[t][n]
                    o = xs[:, t, n * 512:(n + 1) * 512]
                    if coef == 1.0:
                        z = tt(o, ps[:, :], o, ALU.add, w)
                    else:
                        z = stt(o, ps[:, :], coef, o, ALU.mult, ALU.add, w)
                    release(b, z)
                    toks[t, n] = z
            return toks

        everyrow = slice(0, 128)

        def ffn(i, gl, tin, coef):
            F = ffns[i][3]
            nf = len(row_starts(F))
            with ExitStack() as c:
                fh = sb(f"fh{i}", [128, 22, S], F32R, c)
                fl = sb(f"fl{i}", [128, 22, S], F32R, c)
                sg = [sb(f"sg{i}_{j}", [128, 2, 2 * S], c=c) for j in range(2)]
                hr, tcol, row = norm_T(gl, tin)
                tR = None
                parts = [None] * nf
                sg_free = [None, None]

                def post(bb, f, n, w, s, k):
                    m = tt(s[:, :, :], pair(bb), R24, ALU.mult, w, sg_free[k], tR)
                    release(bb[0][0], m)
                    release(bb[1][0], m)
                    a = act(s[:, :, 0:256], s[:, :, 0:256], ACT.Silu, m)
                    yield
                    m = tt(s[:, :, 0:256], s[:, :, 0:256], s[:, :, 256:512], ALU.mult, a)
                    h = act(fh[:, f:f + 2, :], s[:, :, 0:256], ACT.Copy, m)
                    lo = tt(fl[:, f:f + 2, :], s[:, :, 0:256], fh[:, f:f + 2, :].bitcast(F32), ALU.subtract, h)
                    sg_free[k] = lo
                    for j in range(2):
                        sl = slice(64, 128) if (n != 256 and j == 1) else everyrow
                        parts[f + j] = (fh[:, f + j, :], fl[:, f + j, :], sl, lo)

                f = 0
                col = 0
                while col < F:
                    n = min(256, F - col)
                    offs = [0, 128] if n == 256 else [0, n - 128]
                    bb = bank2()
                    i0, wh, wl, sd = take()
                    for j in range(2):
                        tg = up_tile(bb[j][1], 0, wh, wl, n, offs[j], sd, hr, bb[j][2])
                    used(i0, tg)
                    i0, wh, wl, sd = take()
                    for j in range(2):
                        tu = up_tile(bb[j][1], 256, wh, wl, n, offs[j], sd, hr, None)
                    if tR is None:
                        tR = row()
                    k = (f // 2) % 2
                    later.append(post(bb, f, n, tu, sg[k], k))
                    used(i0, tu)
                    f += 2
                    col += n
                flush()
                assert f == nf
                r = down(parts, coef)
            return r

        def run(*gens):
            gens = [g for g in gens]
            while gens:
                for g in list(gens):
                    try:
                        next(g)
                    except StopIteration:
                        gens.remove(g)

        def heads_T(dst, d, H, src, after, scale=None, e="act"):
            toks = []
            for h0 in range(0, H, 2):
                b, ps, f = bank()
                m = min(2, H - h0)
                for j in range(m):
                    for t in range(2):
                        c = (2 * j + t) * 128
                        w = tp(ps[0:d, c:c + 128], src(h0 + j, t), ident, f, after, t_c,
                               sig=(j == m - 1 and t == 1))
                o = dst[:, h0:h0 + m, :].rearrange("p h s -> p (h s)")
                if e == "act":
                    k = {} if scale is None else {"scale": scale}
                    z = act(o, ps[0:d, 0:m * 256], ACT.Copy, w, **k)
                elif scale is None:
                    z = cp(o, ps[0:d, 0:m * 256], w)
                else:
                    z = ts(o, ps[0:d, 0:m * 256], scale, None, ALU.mult, None, w)
                release(b, z)
                toks.append(z)
            return toks

        def attention(name, al, H, qT, kT, vN, mask, scale, ready, dst, sink=None, mult=None):
            sm = [al(f"{name}_sm{i}", [128, 2, 256]) for i in range(3)]
            pt = [al(f"{name}_pt{i}", [128, 512]) for i in range(2)]
            mx = al(f"{name}_mx", [128, 4, 16])
            sm_free, pt_free = [None] * 3, [None] * 2
            done, obank = [None, None], {}

            def group(t, h0, turn):
                nk = 128 * (t + 1)
                i, ip = turn % 3, turn % 2
                b, ps, f = bank()
                w = None
                for j in range(2):
                    w = mm(ps[:, j * 256:j * 256 + nk], qT(h0 + j)[:, t * 128:t * 128 + 128],
                           kT(h0 + j)[:, 0:nk], True, True, f, ready, w)
                c0 = t * 8 + h0
                for j in range(2):
                    z = ttr(sm[i][:, j, 0:nk], ps[:, j * 256:j * 256 + nk], mask(t), scale, -3e38, ALU.add,
                            ALU.max, mx[:, 0, c0 + j:c0 + j + 1], w, sm_free[i], t_c1, ready)
                release(b, z)
                if sink is not None:
                    z = tt(mx[:, 0, c0:c0 + 2], mx[:, 0, c0:c0 + 2], sink[:, h0:h0 + 2], ALU.max, z)
                z = ts(mx[:, 1, c0:c0 + 2], mx[:, 0, c0:c0 + 2], -1.0, None, ALU.mult, None, z)
                yield
                for j in range(2):
                    k = {} if mult is not None else {"accum_out": mx[:, 2, c0 + j:c0 + j + 1]}
                    a = act(sm[i][:, j, 0:nk], sm[i][:, j, 0:nk], ACT.Exp, z, bias=mx[:, 1, c0 + j:c0 + j + 1], **k)
                if mult is not None:
                    for j in range(2):
                        a = ttr(sm[i][:, j, 0:nk], sm[i][:, j, 0:nk], mult(t), 1.0, 0.0, ALU.mult, ALU.add,
                                mx[:, 2, c0 + j:c0 + j + 1], a)
                yield
                b, ps, f = bank()
                for j in range(2):
                    for kt in range(t + 1):
                        o = (j * (t + 1) + kt) * 128
                        w = tp(ps[:, o:o + 128], sm[i][:, j, kt * 128:kt * 128 + 128], ident, f, a, t_c,
                               sig=(j == 1 and kt == t))
                sm_free[i] = w
                z = cp(pt[ip][:, 0:256 * (t + 1)], ps[:, 0:256 * (t + 1)], w, pt_free[ip], e="act")
                release(b, z)
                yield
                if t not in obank:
                    obank[t] = bank()
                ob, ops_, of = obank[t]
                for j in range(2):
                    for kt in range(t + 1):
                        o = (j * (t + 1) + kt) * 128
                        w = mm(ops_[:, (h0 + j) * 64:(h0 + j) * 64 + 64], pt[ip][:, o:o + 128], vN(kt, h0 + j),
                               kt == 0, kt == t, z, of, sig=(j == 1 and kt == t))
                pt_free[ip] = w
                if h0 != H - 2:
                    return
                c0 = t * 8
                l = mx[:, 2, c0:c0 + H]
                tail = a
                if sink is not None:
                    z = tt(mx[:, 3, c0:c0 + H], sink[:, 0:H], mx[:, 1, c0:c0 + H], ALU.add, a)
                    z = act(mx[:, 3, c0:c0 + H], mx[:, 3, c0:c0 + H], ACT.Exp, z)
                    tail = tt(l, l, mx[:, 3, c0:c0 + H], ALU.add, z)
                z = rcp(mx[:, 3, c0:c0 + H], l, tail)
                z = tt(dst[:, t, :].rearrange("p (h e) -> p h e", h=H),
                       ops_[:, 0:H * 64].rearrange("p (h e) -> p h e", h=H),
                       mx[:, 3, c0:c0 + H].unsqueeze(2).broadcast_to([128, H, 64]), ALU.mult, z, w)
                release(ob, z)
                done[t] = z

            todo = [(t, h0) for t in range(2) for h0 in range(0, H, 2)]
            active, turn = [], 0
            while todo or active:
                for g in list(active):
                    if next(g, "end") == "end":
                        active.remove(g)
                if todo:
                    g = group(*todo.pop(0), turn)
                    turn += 1
                    next(g)
                    active.append(g)
                yield
            return done

        def head_norm(name, al, src, H, d, after, sq=None):
            if sq is None:
                sq = al(name + "_sq", [128, 2, H * d])
            r = al(name + "_r", [128, 2, H])
            a = act(sq[:, :, :], src, ACT.Square, after)
            z = red(r[:, :, :], sq[:, :, :].rearrange("p t (h d) -> p t h d", h=H), ALU.add, a)
            z = ts(r[:, :, :], r[:, :, :], 1.0 / d, EPS, ALU.mult, ALU.add, z)
            rf = r[:, :, :].rearrange("p t h -> p (t h)")
            return r, power(rf, rf, 2 * H, z)

        def even_mixer(gl, tin):
            with ExitStack() as c:
                hr, tcol, row = norm_T(gl, tin)
                Q.fence()
                def sbc(name, shape):
                    return sb(name, shape, c=c)

                u = sb("ev_u", [128, 4, PAD + S], c=c)
                acc = sb("ev_acc", [128, 4, S], c=c)
                sq = sb("ev_sqc", [128, 4, S], c=c)
                rs = sb("ev_rs", [128, S], c=c)
                th = [sb(f"ev_th{i}", [128, 2 * S], c=c) for i in range(2)]
                vr = sb("ev_vr", [128, 4], c=c)
                tR = None
                qkv = sb("ev_qkv", [128, 2, 768], c=c)
                qT = sb("ev_qT", [64, 8, S], c=c)
                kT = sb("ev_kT", [64, 2, S], c=c)
                o = sb("ev_o", [128, 2, 512], c=c)
                mh = sb("ev_mh", [128, 8, S], F32R, c)
                ml = sb("ev_ml", [128, 8, S], F32R, c)
                cwr = sb("ev_cwr", [34, 512], c=c)
                cw = sb("ev_cw", [128, 4, 34], c=c)
                cb = sb("ev_cb", [128, 3, 4], c=c)
                qg = sb("ev_qg", [64, 2], c=c)
                sk = sb("ev_sk", [128, 8], c=c)
                z0 = memset(u[:, :, 0:PAD], 0.0)
                fenced = [x for x in Q.pend["act"]]
                Q.waits("act", fenced)
                par(cwr[0:31, :], A["ev_conv_w"][0])
                par(cwr[31:32, :], A["ev_conv_b"])
                par(cwr[32:33, :], A["ev_ln_g"])
                par(cwr[33:34, :], A["ev_ln_b"])
                par(qg[:, 0:1], A["ev_q_norm_g"][0].rearrange("(p a) -> p a", a=1))
                par(qg[:, 1:2], A["ev_k_norm_g"][0].rearrange("(p a) -> p a", a=1))
                tpar = par(sk[:, :], A["ev_sinks"].broadcast_to([128, 8]))
                b, ps, f = bank()
                for j in range(4):
                    w = tp(ps[:, j * 34:(j + 1) * 34], cwr[:, j * 128:(j + 1) * 128], ident[0:34, 0:34], f, tpar, t_c)
                tcw = cp(cw[:, :, :].rearrange("p a b -> p (a b)"), ps[:, 0:136], w)
                release(b, tcw)
                tch = ts(cw[:, :, 0:31], cw[:, :, 0:31], 0.5, None, ALU.mult, None, tcw)

                du = [None] * 4
                for j0 in (0, 2):
                    bb = [bank(), bank()]
                    for c0 in (0, 256):
                        i0, wh, wl, sd = take()
                        tl = [up_tile(bb[j][1], c0, wh, wl, 256, j * 128, sd, hr, bb[j][2]) for j in range(2)]
                        if tR is None and c0:
                            tR = row()
                        used(i0, tl[1])
                    for j in range(2):
                        z = tt(two(th[j][:, :]), two(bb[j][1][:, :]), R22, ALU.mult, tl[j], du[j], tR)
                        release(bb[j][0], z)
                        a = act(th[j][:, 256:512], th[j][:, 256:512], ACT.Tanh, z, scale=0.5)
                        du[j0 + j] = stt(u[:, j0 + j, PAD:], th[j][:, 256:512], 1.0, th[j][:, 0:256], ALU.add, ALU.mult, a)

                def conv():
                    cur = [None] * 4
                    for k in range(CONV_W):
                        o0 = PAD - (CONV_W - 1) + k
                        for j in range(4):
                            src = u[:, j, o0:o0 + S]
                            if k == 0:
                                cur[j] = ts(acc[:, j, :], src, cw[:, j, 0:1], cw[:, j, 31:32], ALU.mult, ALU.add,
                                            du[j], tch, z0)
                            else:
                                cur[j] = stt(acc[:, j, :], src, cw[:, j, k:k + 1], acc[:, j, :], ALU.mult, ALU.add,
                                             cur[j])
                        if k % 2 == 0:
                            yield
                    b, ps, f = bank()
                    for j in range(4):
                        w = mm(ps[:, 0:256], C("ones"), acc[:, j, :], j == 0, j == 3, f, cur[j])
                    yield
                    z = tt(acc[:, :, :], acc[:, :, :], ps[:, 0:256].unsqueeze(1).broadcast_to([128, 4, 256]),
                           ALU.subtract, w)
                    release(b, z)
                    a = act(sq[:, :, :], acc[:, :, :], ACT.Square, z)
                    yield
                    b, ps, f = bank()
                    for t in range(2):
                        for j in range(4):
                            w = mm(ps[:, t:t + 1], sq[:, j, t * 128:t * 128 + 128], C("ones", 0, 1), j == 0, j == 3,
                                   f, a)
                    z2 = ts(vr[:, 0:2], ps[:, 0:2], EPS, None, ALU.add, None, w)
                    release(b, z2)
                    z2 = power(vr[:, 2:4], vr[:, 0:2], 2, z2)
                    for t in range(2):
                        z2 = ts(dg[:, t, :], ident, vr[:, 2 + t:3 + t], 512.0, ALU.mult, ALU.mult, z2)
                    b, ps, f = bank()
                    for t in range(2):
                        w = mm(ps[:, t * 128:t * 128 + 128], C("ones"), dg[:, t, :], True, True, f, z2)
                    z2 = cp(rs[:, :], ps[:, 0:256], w)
                    release(b, z2)
                    z = tt(acc[:, :, :], acc[:, :, :], rs[:, :].unsqueeze(1).broadcast_to([128, 4, 256]), ALU.mult, z2, z)
                    yield
                    for j in range(4):
                        a = act(sq[:, j, :], acc[:, j, :], ACT.Silu, z, scale=cw[:, j, 32:33], bias=cw[:, j, 33:34])
                    fl = "p k s -> p (k s)"
                    a = act(mh[:, 0:4, :], sq[:, :, :], ACT.Copy, a)
                    z = tt(ml[:, 0:4, :], sq[:, :, :], mh[:, 0:4, :].bitcast(F32), ALU.subtract, a)
                    res["u"] = z

                res = {}

                def swa():
                    q0 = x_cols(512, hr)
                    tq = []
                    for t in range(2):
                        z = by_token(qkv[:, t, 0:512], q0[t][1][:, :], t, q0[t][2], tcol)
                        release(q0[t][0], z)
                        tq.append(z)
                    yield
                    q1 = x_cols(256, hr)
                    for t in range(2):
                        z = by_token(qkv[:, t, 512:768], q1[t][1][:, 0:256], t, q1[t][2], tcol)
                        release(q1[t][0], z)
                        tq.append(z)
                    yield
                    r, tr = head_norm("ev_hn", sbc, qkv[:, :, 0:640], 10, 64, tq)
                    v10 = qkv[:, :, 0:640].rearrange("p t (h e) -> p t h e", h=10)
                    z = None
                    for t in range(2):
                        z = tt(v10[:, t], v10[:, t], r[:, t, :].unsqueeze(2).broadcast_to([128, 10, 64]), ALU.mult,
                               tr, z)
                    yield
                    rq = heads_T(qT, 64, 8, lambda h, t: qkv[:, t, h * 64:h * 64 + 64], z, qg[:, 0:1])
                    rk = heads_T(kT, 64, 2, lambda h, t: qkv[:, t, 512 + h * 64:576 + h * 64], z, qg[:, 1:2])
                    yield
                    off = CONSTS["swa"][0]
                    do = yield from attention(
                        "ev_at", sbc, 8, lambda h: qT[:, h, :], lambda h: kT[:, h // 4, :],
                        lambda kt, h: qkv[:, kt, 640 + (h // 4) * 64:704 + (h // 4) * 64],
                        lambda t: cst[:, off + 128 * t:off + 128 * t + 128 * (t + 1)], 0.125, [rq, rk], o, sink=sk)
                    res["o"] = transposed(lambda k, t: o[:, t, k * 128:(k + 1) * 128], 4, mh[:, 4:8, :],
                                          ml[:, 4:8, :], lambda k, t: do[t])

                run(swa(), conv())
                parts = [(mh[:, k, :], ml[:, k, :], everyrow, res["u"] if k < 4 else res["o"][(k - 4) // 2])
                         for k in range(8)]
                r = down(parts, 1.0)
            return r

        def odd_mixer(gl, tin):
            with ExitStack() as c:
                hr, tcol, row = norm_T(gl, tin)
                Q.fence()
                def sbc(name, shape):
                    return sb(name, shape, c=c)

                u = sb("od_u", [128, 4, 16 + S], c=c)
                w1 = [sb(f"od_w{i}", [128, 3, 16 + S], c=c) for i in range(2)]
                pl = sb("od_pl", [128, 4, S], c=c)
                pw = sb("od_pw", [128, 4, 128], c=c)
                psc = sb("od_psc", [128, 4], c=c)
                qkv = sb("od_qkv", [128, 2, 1536], c=c)
                qT = sb("od_qT", [64, 8, S], c=c)
                kT = sb("od_kT", [64, 8, S], c=c)
                mh = sb("od_mh", [128, 8, S], F32R, c)
                ml = sb("od_ml", [128, 8, S], F32R, c)
                qg = sb("od_qg", [64, 2], c=c)
                zs = [memset(u[:, :, 0:16], 0.0), memset(w1[0][:, :, 0:16], 0.0), memset(w1[1][:, :, 0:16], 0.0)]
                Q.waits("act", list(Q.pend["act"]))
                par(pw[:, :, :], A["od_pool_w"][0].rearrange("g c j -> c g j"))
                par(psc[:, :], A["od_pool_scale"][0].rearrange("(g p) -> p g", p=128))
                par(qg[:, 0:1], A["od_q_norm_g"][0].rearrange("(p a) -> p a", a=1))
                tpar = par(qg[:, 1:2], A["od_k_norm_g"][0].rearrange("(p a) -> p a", a=1))
                o = sb("od_o", [128, 2, 512], c=c)
                res = {}
                tq = []
                rr = []
                for g in range(3):
                    q0 = x_cols(512, hr)
                    for t in range(2):
                        z = by_token(qkv[:, t, g * 512:(g + 1) * 512], q0[t][1][:, :], t, q0[t][2], tcol)
                        release(q0[t][0], z)
                        tq.append(z)

                def pool():
                    du = []
                    for j0 in (0, 2):
                        i0, wh, wl, sd = take()
                        b, ps, f = bank()
                        for j in range(2):
                            w = up_tile(ps, 256 * j, wh, wl, 256, j * 128, sd, hr, f)
                        used(i0, w)
                        if j0 == 0:
                            tR = row()
                        a = tt(u[:, j0:j0 + 2, 16:], two(ps[:, :]), R22, ALU.mult, w, tR)
                        release(b, a)
                        du.append(a)
                        yield
                    z = [du, zs]
                    s0 = u
                    lo = 0
                    for step, n in ((1, 4), (2, 3), (4, 2), (8, 1)):
                        g = 4 - n
                        if n == 4:
                            z = tt(pl[:, 0, :], u[:, 0, 16:], u[:, 0, 15:15 + S], ALU.add, z)
                            z = tt(w1[0][:, :, 16:], u[:, 1:4, 16:], u[:, 1:4, 15:15 + S], ALU.add, z)
                            src, k = w1[0], 1
                        else:
                            z = tt(pl[:, g, :], src[:, 3 - n, 16:], src[:, 3 - n, 16 - step:16 - step + S], ALU.add, z)
                            if n > 1:
                                dst = w1[k % 2]
                                z = tt(dst[:, 4 - n:3, 16:], src[:, 4 - n:3, 16:], src[:, 4 - n:3, 16 - step:16 - step + S],
                                       ALU.add, z)
                                src = dst
                                k += 1
                        yield
                    rc = C("rcount").rearrange("p (g s) -> p g s", g=4)
                    z = tt(pl[:, :, 0:16], pl[:, :, 0:16], rc, ALU.mult, z, t_c1)
                    for g in range(4):
                        z = stt(pl[:, g, 16:], pl[:, g, 16:], 1.0 / (2 << g), u[:, g, 32:], ALU.mult, ALU.subtract, z)
                    z = tt(pl[:, :, 0:16], pl[:, :, 0:16], u[:, :, 16:32], ALU.subtract, z)
                    yield
                    for g in range(4):
                        b, ps, f = bank()
                        w = mm(ps[:, 0:256], pw[:, g, :], pl[:, g, :], True, True, f, z, tpar)
                        a = act(mh[:, 4 + g, :], ps[:, 0:256], ACT.Copy, w, tpar, scale=psc[:, g:g + 1])
                        d = stt(ml[:, 4 + g, :], ps[:, 0:256], psc[:, g:g + 1], mh[:, 4 + g, :].bitcast(F32),
                                ALU.mult, ALU.subtract, a)
                        release(b, d)
                    res["u"] = d

                def dil():
                    r, tr = head_norm("od_hn", sbc, qkv[:, :, 0:1024], 16, 64, tq)
                    yield
                    z = None
                    for t in range(2):
                        v = qkv[:, t, 0:1024].rearrange("p (h e) -> p h e", h=16)
                        z = tt(v, v, r[:, t, :].unsqueeze(2).broadcast_to([128, 16, 64]), ALU.mult, tr, z)
                    yield
                    rq = heads_T(qT, 64, 8, lambda h, t: qkv[:, t, h * 64:h * 64 + 64], [z, tpar], qg[:, 0:1])
                    yield
                    rk = heads_T(kT, 64, 8, lambda h, t: qkv[:, t, 512 + h * 64:576 + h * 64], [z, tpar], qg[:, 1:2])
                    yield
                    off, of2 = CONSTS["dil"][0], CONSTS["mult"][0]
                    do = yield from attention(
                        "od_at", sbc, 8, lambda h: qT[:, h, :], lambda h: kT[:, h, :],
                        lambda kt, h: qkv[:, kt, 1024 + h * 64:1088 + h * 64],
                        lambda t: cst[:, off + 128 * t:off + 128 * t + 128 * (t + 1)], 0.125, [rq, rk], o,
                        mult=lambda t: cst[:, of2 + 128 * t:of2 + 128 * t + 128 * (t + 1)])
                    res["o"] = transposed(lambda k, t: o[:, t, k * 128:(k + 1) * 128], 4, mh[:, 0:4, :],
                                          ml[:, 0:4, :], lambda k, t: do[t])

                run(dil(), pool())
                parts = [(mh[:, k, :], ml[:, k, :], everyrow, res["u"] if k >= 4 else res["o"][k // 2])
                         for k in range(8)]
                r = down(parts, 1.0)
            return r

        def rope_tables(cs, sn, c):
            pi_ = sb("rp_i", [128, 2], I32, c)
            pf = sb("rp_f", [128, 2], c=c)
            w = [sb(f"rp_w{i}", [128, 2, 16], c=c) for i in range(4)]
            tpar = par(pi_[:, :], A["positions_2"][0].rearrange("(t p) -> p t", p=128))
            z = cp(pf[:, :], pi_[:, :], tpar)
            for t in range(2):
                z = ts(w[0][:, t, :], C("invf"), pf[:, t:t + 1], None, ALU.mult, None, z, t_c)
            magic = 12582912.0
            z = ts(w[1][:, :, :], w[0][:, :, :], 1.0 / (2 * np.pi), magic, ALU.mult, ALU.add, z)
            z = ts(w[1][:, :, :], w[1][:, :, :], -magic, None, ALU.add, None, z)
            c1 = 6.28125
            c2 = float(np.float32(np.round((2 * np.pi - c1) * 2 ** 20) / 2 ** 20))
            c3 = float(2 * np.pi - c1 - c2)
            for k in (c1, c2, c3):
                z = stt(w[0][:, :, :], w[1][:, :, :], -k, w[0][:, :, :], ALU.mult, ALU.add, z)
            top = 3.1415925
            z = ts(w[0][:, :, :], w[0][:, :, :], top, -top, ALU.min, ALU.max, z)
            a = act(sn, w[0][:, :, :], ACT.Sin, z)
            z = ts(w[2][:, :, :], w[0][:, :, :], -1.0, None, ALU.mult, None, z)
            z = tt(w[2][:, :, :], w[2][:, :, :], w[0][:, :, :], ALU.max, z)
            z = ts(w[3][:, :, :], w[2][:, :, :], -1.0, float(np.pi / 2), ALU.mult, ALU.add, z)
            return act(cs, w[3][:, :, :], ACT.Sin, z, a)

        def mixer2(l, gl, tin, csn, t_rope):
            P = f"m{l}_"
            with ExitStack() as c:
                hr, tcol, row = norm_T(gl, tin)
                Q.fence()
                W0 = 416
                nat = sb(P + "nat", [128, 2, 1880], c=c)
                G = sb(P + "G", [128, 32, S], c=c)
                bh = sb(P + "bh", [128, 8, S], F32R, c)
                bl = sb(P + "bl", [128, 8, S], F32R, c)
                cvw = sb(P + "cvw", [128, 2, 3], c=c)
                gup = sb(P + "gup", [16, 128], c=c)
                gbg = sb(P + "gbg", [128, 1], c=c)
                gng = sb(P + "gng", [128, 64], c=c)
                qng = sb(P + "qng", [128, 2], c=c)
                kng = sb(P + "kng", [128, 1], c=c)
                SCR = 12320
                scr = sb(P + "scr", [128, SCR], c=c)
                R_DSA, R_GLA = (0, 6240), (6240, SCR)
                Q.waits("act", list(Q.pend["act"]))
                if l == 0:
                    Q.dma("act", cst[:, KEEP:KEEP + SECOND], A["consts"][:, FIRST:FIRST + SECOND], s_c, 32, t_c1)
                tc2 = (s_c, 32)
                for t in range(2):
                    par(cvw[:, t, :], A["conv_w_2"][l][:, t * 128:(t + 1) * 128].rearrange("k p -> p k"))
                par(gup[:, :], A["gla_w_gate_up_2"][l])
                par(gbg[:, :], A["gla_b_gate_2"][l].rearrange("(p a) -> p a", a=1))
                par(gng[:, :], A["gla_norm_g_2"][l].rearrange("(a n) -> a n", a=1).broadcast_to([128, 64]))
                par(qng[:, :], A["mla_q_norm_g_2"][l].rearrange("(k p) -> p k", p=128))
                tpar = par(kng[:, :], A["mla_kv_norm_g_2"][l].rearrange("(p a) -> p a", a=1))

                tn = {}
                at = 0
                for g, (c0, n) in enumerate(X2):
                    q0 = x_cols(n, hr)
                    for t in range(2):
                        z = by_token(nat[:, t, at:at + n], q0[t][1][:, 0:n], t, q0[t][2], tcol, e="act" if t else "dve")
                        release(q0[t][0], z)
                        tn[g, t] = z
                    at += n
                tnat = [tn[k] for k in tn]

                def N(a, b, t=None):
                    return nat[:, :, W0 + a:W0 + b] if t is None else nat[:, t, W0 + a:W0 + b]

                res = {}

                def gates():
                    tR = row()
                    if True:
                        cT, y = G[:, 0:2, :], G[:, 2:4, :]
                        uu = G[:, 4:8, :].rearrange("p a s -> p (a s)")[:, 0:2 * (2 + S)]\
                            .rearrange("p (a s) -> p a s", a=2)
                        z0 = memset(uu[:, :, 0:2], 0.0)
                        bks = []
                        for g in range(3):
                            i0, wh, wl, sd = take()
                            b, ps, f = bank()
                            for j in range(2):
                                w = up_tile(ps, 256 * j, wh, wl, 256, j * 128, sd, hr, f)
                            used(i0, w)
                            bks.append((b, ps[:, :].rearrange("p (a s) -> p a s", a=2), w))
                            yield
                        z = tt(cT[:, :, :], bks[1][1], R22, ALU.mult, bks[1][2], tR)
                        release(bks[1][0], z)
                        z = tt(cT[:, :, :], cT[:, :, :], R22, ALU.mult, z)
                        z = tt(uu[:, :, 2:], bks[2][1], cT[:, :, :], ALU.mult, bks[2][2], z)
                        release(bks[2][0], z)
                        yield
                        for j in range(2):
                            z = ts(y[:, j, :], uu[:, j, 0:S], cvw[:, j, 0:1], None, ALU.mult, None, z, z0, tpar)
                            for k in (1, 2):
                                z = stt(y[:, j, :], uu[:, j, k:k + S], cvw[:, j, k:k + 1], y[:, j, :], ALU.mult,
                                        ALU.add, z)
                        z = tt(y[:, :, :], y[:, :, :], bks[0][1], ALU.mult, z, bks[0][2])
                        release(bks[0][0], z)
                        z = tt(y[:, :, :], y[:, :, :], R22, ALU.mult, z)
                        a = act(bh[:, 2:4, :], y[:, :, :], ACT.Copy, z)
                        res[1] = tt(bl[:, 2:4, :], y[:, :, :], bh[:, 2:4, :].bitcast(F32), ALU.subtract, a)
                    yield
                    tg = {}
                    for n, merge in FILL:
                        if not merge:
                            for g in range(4 * n, 4 * n + 4):
                                i0, wh, wl, sd = take()
                                b, ps, f = bank()
                                for j in range(2):
                                    w = up_tile(ps, 256 * j, wh, wl, 256, j * 128, sd, hr, f)
                                used(i0, w)
                                gg = G[:, 2 * g:2 * g + 2, :]
                                z = tt(gg, two(ps[:, :]), R22, ALU.mult, w, res[1], tR)
                                release(b, z)
                                tg[g] = act(gg, gg, ACT.Tanh, z, scale=0.5)
                                yield
                            continue
                        while n not in res:
                            yield
                        i0, wh, wl, sd = take()
                        for q4 in range(4):
                            b, ps, f = bank()
                            for j in range(2):
                                fcol = (2 * q4 + j) * 128
                                for kk in range(2):
                                    w = mm3(ps[:, 256 * j:256 * j + 256],
                                            wh[:, kk * 1024 + fcol:kk * 1024 + fcol + 128],
                                            wl[:, kk * 1024 + fcol:kk * 1024 + fcol + 128], bh[:, 2 * n + kk, :],
                                            bl[:, 2 * n + kk, :], kk == 0, kk == 1, f, sd, res[n], sig=(kk == 1))
                            g = G[:, 8 * n + 2 * q4:8 * n + 2 * q4 + 2, :]
                            z = stt(g, g, 1.0, two(ps[:, :]), ALU.add, ALU.mult, w, tg[4 * n + q4])
                            release(b, z)
                            if n != 1:
                                o_ = G[:, 8 + 2 * q4:8 + 2 * q4 + 2, :]
                                z = tt(o_, o_, g, ALU.add, z, res["acc", q4], e="pool" if n else "dve")
                            res["acc", q4] = z
                            if q4 % 2:
                                yield
                        used(i0, w)

                def finish(n, o, do):
                    res[n] = transposed(lambda k, t: o[:, t, k * 128:(k + 1) * 128], 2, bh[:, 2 * n:2 * n + 2, :],
                                        bl[:, 2 * n:2 * n + 2, :], lambda k, t: do[t])

                def causal(t):
                    off = CONSTS["causal"][0]
                    return cst[:, off + 128 * t:off + 128 * t + 128 * (t + 1)]

                def mla():
                    if True:
                        cc = Region(scr, 0, SCR)
                        wq = cc(P + "wq", [128, 2, 384])
                        wkv = cc(P + "wkv", [128, 512])
                        Q.waits("act", list(Q.pend["act"]))
                        par(wq, A["mla_w_q_up_2"][l].rearrange("(k p) n -> p k n", p=128))
                        tpw = par(wkv, A["mla_w_kv_up_2"][l])
                        cqT = cc(P + "cqT", [128, 3, S])
                        qn = cc(P + "qn", [128, 2, 384])
                        kn = cc(P + "kn", [128, 2, 384])
                        vn = cc(P + "vn", [128, 2, 256])
                        qT = cc(P + "qT", [96, 4, S])
                        kT = cc(P + "kT", [96, 4, S])
                        rw = [cc(P + f"rw{i}", [128, 2, 64]) for i in range(4)]
                        r, tr = head_norm(P + "cq", cc, nat[:, :, 0:256], 1, 256, tnat)
                        r2, tr2 = head_norm(P + "ck", cc, nat[:, :, 256:384], 1, 128, tnat)
                        z = None
                        for t in range(2):
                            z = ts(nat[:, t, 0:256], nat[:, t, 0:256], r[:, t, 0:1], None, ALU.mult, None, tr, z)
                            z = ts(nat[:, t, 256:384], nat[:, t, 256:384], r2[:, t, 0:1], None, ALU.mult, None, tr2, z)
                        yield
                        b, ps, f = bank()
                        b2, ps2, f2 = bank()
                        for k in range(3):
                            for t in range(2):
                                o = (ps if k < 2 else ps2)[:, (2 * (k % 2) + t) * 128:(2 * (k % 2) + t) * 128 + 128]
                                w = tp(o, nat[:, t, k * 128:k * 128 + 128], ident, f, f2, z)
                        for k in range(3):
                            g = qng[:, k:k + 1] if k < 2 else kng[:, 0:1]
                            p_ = (ps if k < 2 else ps2)[:, 256 * (k % 2):256 * (k % 2) + 256]
                            a = act(cqT[:, k, :], p_, ACT.Copy, w, tpar, scale=g)
                        release(b, a)
                        release(b2, a)
                        yield
                        zz = []
                        for t in range(2):
                            sl = slice(t * 128, t * 128 + 128)
                            b, ps, f = bank()
                            for k in range(2):
                                w = mm(ps[:, 0:384], cqT[:, k, sl], wq[:, k, :], k == 0, k == 1, f, a, tpw)
                            z = cp(qn[:, t, :], ps[:, 0:384], w, e="act")
                            release(b, z)
                            b, ps, f = bank()
                            w = mm(ps[:, :], cqT[:, 2, sl], wkv[:, :], True, True, f, a)
                            pv = ps[:, :].rearrange("p (h e) -> p h e", h=4)
                            z1 = cp(kn[:, t, :].rearrange("p (h e) -> p h e", h=4)[:, :, 0:64], pv[:, :, 0:64], w)
                            z2 = cp(vn[:, t, :].rearrange("p (h e) -> p h e", h=4), pv[:, :, 64:128], z1)
                            release(b, z2)
                            zz += [z, z1, z2]
                        yield
                        z = [zz, t_rope]
                        cs, sn = csn

                        def b4(x):
                            return x.unsqueeze(1).broadcast_to([128, 4, 16])

                        for t in range(2):
                            q4 = qn[:, t, :].rearrange("p (h e) -> p h e", h=4)
                            x1, x2 = q4[:, :, 64:80], q4[:, :, 80:96]
                            v = [rw[i][:, t, :].rearrange("p (h e) -> p h e", h=4) for i in range(4)]
                            ct, st = b4(cs[:, t, :]), b4(sn[:, t, :])
                            za = tt(v[0], x1, ct, ALU.mult, z)
                            zb = tt(v[1], x2, st, ALU.mult, z)
                            zc = tt(v[2], x1, st, ALU.mult, z)
                            zd = tt(v[3], x2, ct, ALU.mult, z)
                            z1 = tt(x1, v[0], v[1], ALU.subtract, zd)
                            zq = tt(x2, v[2], v[3], ALU.add, z1)
                            kr = nat[:, t, 384:416]
                            k1, k2 = kr[:, 0:16], kr[:, 16:32]
                            c_, s_ = cs[:, t, :], sn[:, t, :]
                            m = [rw[i][:, t, 0:16] for i in range(4)]
                            za = tt(m[0], k1, c_, ALU.mult, zq)
                            zb = tt(m[1], k2, s_, ALU.mult, zq)
                            zc = tt(m[2], k1, s_, ALU.mult, zq)
                            zd = tt(m[3], k2, c_, ALU.mult, zq)
                            k4 = kn[:, t, :].rearrange("p (h e) -> p h e", h=4)
                            z1 = tt(k4[:, :, 64:80], b4(m[0]), b4(m[1]), ALU.subtract, zd)
                            zk = tt(k4[:, :, 80:96], b4(m[2]), b4(m[3]), ALU.add, z1)
                            z = [zk]
                            yield
                        rq = heads_T(qT, 96, 4, lambda h, t: qn[:, t, h * 96:h * 96 + 96], z)
                        yield
                        rk = heads_T(kT, 96, 4, lambda h, t: kn[:, t, h * 96:h * 96 + 96], z)
                        yield
                        o = nat[:, :, 0:256]
                        do = yield from attention(
                            P + "mat", cc, 4, lambda h: qT[:, h, :], lambda h: kT[:, h, :],
                            lambda kt, h: vn[:, kt, h * 64:h * 64 + 64], causal, 96 ** -0.5, [rq, rk, tc2], o)
                        finish(0, o, do)

                def dsa():
                    if True:
                        cc = Region(scr, *R_DSA)
                        iqT = cc(P + "iqT", [128, 2, S])
                        ikT = cc(P + "ikT", [128, 1, S])
                        ik4 = cc(P + "ik4", [128, 2, 128])
                        rl = [cc(P + f"rl{i}", [128, 512]) for i in range(2)]
                        sc = cc(P + "sc", [128, 384])
                        iw = cc(P + "iw", [128, 2, 8])
                        m8 = cc(P + "m8", [128, 8])
                        qT = cc(P + "dqT", [128, 2, S])
                        kT = cc(P + "dkT", [128, 1, S])
                        dk2 = cc(P + "dk2", [128, 2, 128])
                        z1, z2 = [], []
                        for t in range(2):
                            z1.append(cp(ik4[:, t, :].rearrange("p (a e) -> p a e", a=4),
                                         N(640, 672, t).unsqueeze(1).broadcast_to([128, 4, 32]), tnat))
                            z2.append(cp(dk2[:, t, :].rearrange("p (a e) -> p a e", a=2),
                                         N(256, 320, t).unsqueeze(1).broadcast_to([128, 2, 64]), tnat))
                        ri = heads_T(iqT, 128, 2, lambda h, t: N(384 + h * 128, 512 + h * 128, t), tnat)
                        yield
                        rk = heads_T(ikT, 128, 1, lambda h, t: ik4[:, t, :], z1)
                        ti = ts(iw[:, :, :], N(672, 680), 8.0 ** -0.5, None, ALU.mult, None, tnat)
                        yield
                        rq = heads_T(qT, 128, 2, lambda h, t: N(h * 128, h * 128 + 128, t), tnat)
                        rkk = heads_T(kT, 128, 1, lambda h, t: dk2[:, t, :], z2)
                        yield
                        rf = [None, None]
                        masks = []
                        for t in range(2):
                            nk = 128 * (t + 1)
                            s_ = sc[:, 128 * t:128 * t + nk]
                            z = ti
                            for h0 in range(0, 8, 2):
                                i = (h0 // 2) % 2
                                b, ps, f = bank()
                                w = None
                                for j in range(2):
                                    rows = slice(32 * ((h0 + j) % 4), 32 * ((h0 + j) % 4) + 32)
                                    w = mm(ps[:, j * nk:(j + 1) * nk], iqT[rows, h0 // 4, t * 128:t * 128 + 128],
                                           ikT[rows, 0, 0:nk], True, True, f, ri, rk, w)
                                a = act(rl[i][:, 0:2 * nk], ps[:, 0:2 * nk], ACT.Relu, w, rf[i], scale=32.0 ** -0.5)
                                release(b, a)
                                for j in range(2):
                                    first = causal(t) if h0 + j == 0 else s_
                                    z = stt(s_, rl[i][:, j * nk:(j + 1) * nk], iw[:, t, h0 + j:h0 + j + 1], first,
                                            ALU.mult, ALU.add, a, z, tc2)
                                rf[i] = z
                                yield
                            for r_ in range(8):
                                z = op("dve", lambda g, s_=s_: g.max(m8[:, :], s_), z)
                                z = op("dve", lambda g, s_=s_: g.match_replace(s_, m8[:, :], s_, TAKEN), z)
                                if r_ % 2:
                                    yield
                            z = ts(s_, s_, -2e38, NEG, ALU.is_gt, ALU.mult, z)
                            z = tt(s_, s_, causal(t), ALU.add, z)
                            masks.append(z)
                            yield
                        o = N(0, 256)
                        do = yield from attention(
                            P + "dat", cc, 4, lambda h: qT[64 * (h % 2):64 * (h % 2) + 64, h // 2, :],
                            lambda h: kT[64 * (h % 2):64 * (h % 2) + 64, 0, :],
                            lambda kt, h: N(320, 384, kt), lambda t: sc[:, 128 * t:128 * t + 128 * (t + 1)],
                            0.125, [rq, rkk, masks], o)
                        finish(2, o, do)

                def gla():
                    if True:
                        cc = Region(scr, *R_GLA)
                        B = {}

                        def buf(n, shape=(128, S)):
                            B[n] = cc(P + "g_" + n, list(shape))
                            return B[n]

                        qT, kT, cum, e1, e2 = (buf(n) for n in ("q", "k", "cum", "e1", "e2"))
                        glT = buf("gl", (16, S))
                        qz = buf("qz", (128, 4, 128))
                        kq = buf("kq", (128, 4, S))
                        kl, ql = [kq[:, 0, :], kq[:, 1, :]], [kq[:, 2, :], kq[:, 3, :]]
                        at = buf("at", (128, 2, 4, 128))
                        kd = buf("kd", (128, 2, 128))
                        st = buf("st", (128, 3, 256))
                        um = buf("um", (128, 256))
                        o = buf("o", (128, 2, 256))
                        og = kq[:, 2:4, :]
                        el = buf("el", (128, 4))
                        z0 = memset(qz[:, :, :], 0.0)
                        z1 = memset(at[:, :, :, :], 0.0)
                        b, ps, f = bank()
                        for j, a0 in enumerate((680, 808)):
                            for t in range(2):
                                w = tp(ps[:, (2 * j + t) * 128:(2 * j + t) * 128 + 128], N(a0, a0 + 128, t), ident, f,
                                       tnat)
                        tq = act(qT[:, :], ps[:, 0:256], ACT.Copy, w, scale=32.0 ** -0.5)
                        tk = act(kT[:, :], ps[:, 256:512], ACT.Copy, w)
                        release(b, tk)
                        b, ps, f = bank()
                        for t in range(2):
                            w = tp(ps[0:16, t * 128:t * 128 + 128], N(1192, 1208, t), ident, f, tnat)
                        a = cp(glT[:, :], ps[0:16, 0:256], w)
                        release(b, a)
                        yield
                        b, ps, f = bank()
                        w = mm(ps[:, 0:256], gup[:, :], glT[:, :], True, True, f, a, tpar)
                        z = ts(cum[:, :], ps[:, 0:256], gbg[:, 0:1], None, ALU.add, None, w, tpar)
                        release(b, z)
                        zz = z
                        z = ts(e1[:, :], cum[:, :], -1.0, None, ALU.mult, None, z)
                        z = tt(e1[:, :], e1[:, :], cum[:, :], ALU.max, z)
                        a = act(e1[:, :], e1[:, :], ACT.Exp, z, scale=-1.0)
                        a = act(e1[:, :], e1[:, :], ACT.Ln, a, bias=1.0)
                        z = ts(cum[:, :], cum[:, :], 0.0, None, ALU.min, None, a)
                        z = tt(e1[:, :], cum[:, :], e1[:, :], ALU.subtract, z)
                        z = ts(e1[:, :], e1[:, :], 1.0 / 16, None, ALU.mult, None, z)
                        yield
                        zc = memset(e2[:, :], 0.0, z, e="dve")
                        for cch in range(4):
                            sl = slice(cch * 64, cch * 64 + 64)
                            z = op("dve", lambda g, sl=sl: g.tensor_tensor_scan(cum[:, sl], e1[:, sl], e2[:, sl], 0.0,
                                                                               ALU.add, ALU.add), zc)
                        tc = z
                        yield
                        a = act(e1[:, :], cum[:, :], ACT.Exp, tc)
                        cq = cum[:, :].rearrange("p (c s) -> p c s", c=4)
                        for cch in range(4):
                            o0 = 64 * (cch % 2)
                            z = tt(qz[:, cch, o0:o0 + 64], qT[:, cch * 64:cch * 64 + 64], e1[:, cch * 64:cch * 64 + 64],
                                   ALU.mult, a, tq, z0)
                        z = cp(el[:, :], e1[:, :].rearrange("p (c s) -> p c s", c=4)[:, :, 63], z)
                        tqz = z
                        z = tt(e2[:, :].rearrange("p (c s) -> p c s", c=4), cq[:, :, 63:64].broadcast_to([128, 4, 64]),
                               cq, ALU.subtract, z)
                        a = act(e2[:, :], e2[:, :], ACT.Exp, z)
                        z = tt(e2[:, :], e2[:, :], kT[:, :], ALU.mult, a, tk)
                        yield
                        b, ps, f = bank()
                        for t in range(2):
                            w = tp(ps[:, t * 128:t * 128 + 128], e2[:, t * 128:t * 128 + 128], ident, f, z)
                        tkd = cp(kd[:, :, :].rearrange("p a b -> p (a b)"), ps[:, 0:256], w)
                        release(b, tkd)
                        yield
                        tst = []
                        zprev = None
                        for cch in range(3):
                            t, p0 = cch // 2, 64 * (cch % 2)
                            b, ps, f = bank()
                            w = mm(ps[:, 0:256], kd[p0:p0 + 64, t, :], N(936, 1192, t)[p0:p0 + 64, :], True, True, f,
                                   tkd, tnat)
                            if cch == 0:
                                z = tt(st[:, 0, :], ps[:, 0:256], C("block"), ALU.mult, w, tc2)
                                release(b, z)
                            else:
                                z = tt(um[:, :], ps[:, 0:256], C("block"), ALU.mult, w, zprev)
                                release(b, z)
                                z = stt(st[:, cch, :], st[:, cch - 1, :], el[:, cch:cch + 1], um[:, :], ALU.mult,
                                        ALU.add, z, zprev, tqz)
                            zprev = z
                            tst.append(z)
                            yield
                        lv_free = [None, None]
                        tat = z1
                        for lev in range(7):
                            i = lev % 2
                            if lev == 0:
                                qq, kk = qT, kT
                                zl = [tq, tk]
                            else:
                                s_ = 1 << (lev - 1)
                                n2 = S // (2 * s_)
                                cv = cum[:, :].rearrange("p (n s) -> p n s", s=2 * s_)
                                ev_ = e1[:, :].rearrange("p (n s) -> p n s", s=2 * s_)
                                refb = cv[:, :, s_ - 1:s_].broadcast_to([128, n2, s_])
                                za = tt(ev_[:, :, 0:s_], refb, cv[:, :, 0:s_], ALU.subtract, tc, tqz, lv_free)
                                zb = tt(ev_[:, :, s_:], cv[:, :, s_:], refb, ALU.subtract, za)
                                a = act(e1[:, :], e1[:, :], ACT.Exp, zb)
                                qq, kk = ql[i], kl[i]
                                zq = tt(qq[:, :], qT[:, :], e1[:, :], ALU.mult, a, tq)
                                zk = tt(kk[:, :], kT[:, :], e1[:, :], ALU.mult, a, tk)
                                zl = [zq, zk]
                            yield
                            for t in range(2):
                                bs = [bank() for _ in range(2)]
                                for h in range(4):
                                    sl = slice(t * 128, t * 128 + 128)
                                    b, ps, f = bs[h // 2]
                                    w = mm(ps[:, (h % 2) * 128:(h % 2) * 128 + 128], kk[32 * h:32 * h + 32, sl],
                                           qq[32 * h:32 * h + 32, sl], True, True, f, zl, *( [w] if h % 2 else []))
                                    if h % 2:
                                        lm = C("levels", 128 * lev, 128).bitcast(I32).unsqueeze(1)\
                                            .broadcast_to([128, 2, 128])
                                        z = op("dve", lambda g, o_=at[:, t, h - 1:h + 1, :], lm=lm,
                                               d_=ps[:, 0:256].rearrange("p (a s) -> p a s", a=2):
                                               g.copy_predicated(o_, lm, d_), w, tat, tc2)
                                        tat = z
                                        release(b, z)
                            lv_free = [w, z]
                            yield
                        do = []
                        for t in range(2):
                            b, ps, f = bank()
                            first = True
                            for cch in (2 * t, 2 * t + 1):
                                if cch == 0:
                                    continue
                                w = mm(ps[:, 0:256], qz[:, cch, :], st[:, cch - 1, :], first, False, f, tqz,
                                       tst[cch - 1], sig=False)
                                first = False
                            for h in range(4):
                                w = mm(ps[:, h * 64:h * 64 + 64], at[:, t, h, :], N(936 + h * 64, 1000 + h * 64, t),
                                       False, h == 3, tat, sig=(h == 3))
                            z = cp(o[:, t, :], ps[:, 0:256], w, e="act")
                            release(b, z)
                            do.append(z)
                        yield
                        r, tr = head_norm(P + "gn", cc, o[:, :, :], 4, 64, do, sq=kq[:, 0:2, :])
                        grv = N(1208, 1464)
                        a = act(og[:, :, :], grv, ACT.Tanh, tnat, do, scale=0.5)
                        z = stt(og[:, :, :], og[:, :, :], 1.0, grv, ALU.add, ALU.mult, a)
                        z = ts(og[:, :, :], og[:, :, :], 0.5, None, ALU.mult, None, z)
                        for t in range(2):
                            ov = o[:, t, :].rearrange("p (h e) -> p h e", h=4)
                            z = tt(ov, ov, r[:, t, :].unsqueeze(2).broadcast_to([128, 4, 64]), ALU.mult, tr, z)
                            z = tt(ov, ov, gng[:, :].unsqueeze(1).broadcast_to([128, 4, 64]), ALU.mult, z, tpar)
                        z = tt(o[:, :, :], o[:, :, :], og[:, :, :], ALU.mult, z)
                        yield
                        finish(3, o, [z, z])

                def one_by_one():
                    left["gla"] = True

                    def counted():
                        yield from gla()
                        left["gla"] = False

                    other = counted()
                    for _ in dsa():
                        next(other, None)
                        yield
                    for _ in other:
                        yield
                    Q.fence()
                    yield from mla()

                left = {}
                run(gates(), one_by_one())
                last_pe = Q.last("pe")
                parts = []
                for q4 in range(4):
                    src = G[:, 8 + 2 * q4:8 + 2 * q4 + 2, :].rearrange("p a s -> p (a s)")
                    hh = bh[:, 2 * q4:2 * q4 + 2, :].rearrange("p a s -> p (a s)")
                    ll = bl[:, 2 * q4:2 * q4 + 2, :].rearrange("p a s -> p (a s)")
                    a = act(hh, src, ACT.Copy, res["acc", q4], last_pe, scale=0.5)
                    z = stt(ll, src, 0.5, hh.bitcast(F32), ALU.mult, ALU.subtract, a)
                    parts += [(bh[:, 2 * q4 + j, :], bl[:, 2 * q4 + j, :], everyrow, z) for j in range(2)]
                r = down(parts, 1.0)
            return r

        b, ps, f = bank()
        for k in range(8):
            w = tp(ps[:, 16 * k:16 * k + 10], grow[:, k * 128:k * 128 + 128], ident[0:10, 0:10], f, t_g, t_c)
        t_gc = cp(gcol[:, :, 0:10], ps[:, 0:128].rearrange("p (k g) -> p k g", k=8)[:, :, 0:10], w, e="act")
        release(b, t_gc)

        for _ in range(NH):
            issue_split()

        cs, sn = rope[:, 0], rope[:, 1]
        t_rope = rope_tables(cs, sn, cr)
        fin = stage[0][:, :].rearrange("p (t d) -> p t d", t=2)
        t = t_x
        stages = [lambda t: ffn(0, 0, t, 0.5), lambda t: even_mixer(1, t), lambda t: ffn(1, 2, t, 0.5),
                  lambda t: ffn(2, 3, t, 0.5), lambda t: odd_mixer(4, t), lambda t: ffn(3, 5, t, 0.5)]
        for l in range(2):
            stages += [lambda t, l=l: mixer2(l, 6 + 2 * l, t, (cs, sn), t_rope),
                       lambda t, l=l: ffn(4 + l, 7 + 2 * l, t, 1.0)]
        for s in stages[frm:upto]:
            if s is not stages[0]:
                cr.close()
            t = s(t)
        src, done = xs, [[t[h, 0], t[h, 1]] for h in range(2)]
        if upto >= len(stages):
            src = fin
            gfin = stage[1][:, 0:D]
            t_gf = par(gfin, A["final_norm_g_2"].rearrange("(a n) -> a n", a=1).broadcast_to([128, D]), stage_free)
            tcol = rms_col(t)
            done = [[stt(fin[:, h, :], xs[:, h, :], st8[:, 4 + h:5 + h], gfin[:, :], ALU.mult, ALU.mult, tcol, t_gf)]
                    for h in range(2)]
        for h in range(2):
            Q.dma("act", out[0].rearrange("(t p) d -> p t d", p=128)[:, h, :], src[:, h, :], s_o, 16 * (h + 1), done[h])
        Q.waits("act", [(s_o, 32)])
        if upto < len(stages):
            Q.waits("sp", [x for x in stage_ready.values()][-NS:])
        block = ctx.enter_context(nc.Block())
        Q.emit(block)


def kernel(**inputs):
    import numpy as _np
    import concourse.bacc as _bacc
    from concourse import mybir as _mybir
    from concourse.bass_utils import run_bass_kernel_spmd as _run

    nc = _bacc.Bacc("TRN2", target_bir_lowering=False, num_devices=1)
    arrays, A = {}, {}
    given = dict(inputs)
    given["consts"] = CONST_ARRAY
    for name, a in given.items():
        a = _np.ascontiguousarray(a)
        arrays[f"in_{name}"] = a
        A[name] = nc.dram_tensor(f"in_{name}", a.shape, _mybir.dt.from_np(a.dtype), kind="ExternalInput").ap()
    out = nc.dram_tensor("out_0", (1, S, D), F32, kind="ExternalOutput").ap()
    build(nc, A, out)
    r = _run(nc, [arrays], core_ids=[0])
    return r.results[0]["out_0"]
```

```python
import itertools
from contextlib import ExitStack

import numpy as np
import concourse.bass as bass
from concourse import mybir

F32 = mybir.dt.float32
F32R = mybir.dt.float32r
I32 = mybir.dt.int32
ALU = mybir.AluOpType
ACT = mybir.ActivationFunctionType
AX = mybir.AxisListType.X

D = 1024
KD = 8
S = 256
F1 = 2752
F2 = 2816
EPS = 1e-6
NEG = -1e30
TAKEN = -3e38
CH = 2048
NS = 3
NH = 2
CONV_W = 31
SIDE = 10
SIDE_RATE = 1
OD_Y = 5
EV_Y = 2
PAD = 32

CONSTS = {}


def _consts():
    parts = []

    def put(name, a):
        a = np.ascontiguousarray(a, dtype=np.float32).reshape(128, -1)
        CONSTS[name] = (sum(p.shape[1] for p in parts), a.shape[1])
        parts.append(a)

    put("ident", np.eye(128))
    put("ones", np.full((128, 128), 1.0 / 512))
    half = 16
    inv = (np.float32(10000.0) ** (-np.arange(half, dtype=np.float32) / np.float32(half))).astype(np.float32)
    put("invf", np.broadcast_to(inv, (128, half)))
    q = np.arange(128)[:, None]
    dist = [q - np.arange(128)[None, :], q + 128 - np.arange(256)[None, :]]

    def both(f):
        return np.concatenate([f(d) for d in dist], axis=1)

    def hide(ok):
        return np.where(ok, 0.0, NEG)

    keep = sum(p.shape[1] for p in parts)
    put("swa", both(lambda d: hide((d >= 0) & (d <= 127))))
    put("dil", both(lambda d: hide((d >= 0) & ((d <= 128) | (d % 4 == 0)))))
    put("mult", both(lambda d: np.where(d >= 0, (d <= 128) * 1.0 + (d % 4 == 0) + (d % 16 == 0), 0.0)))
    rc = np.ones((4, 16))
    for g, w in enumerate((2, 4, 8, 16)):
        rc[g] = 1.0 / np.minimum(np.arange(1, 17), w)
    put("rcount", np.broadcast_to(rc.reshape(1, -1), (128, 64)))
    first = np.concatenate(parts, axis=1)
    del parts[1:]
    parts[0] = first[:, 0:keep]
    put("causal", both(lambda d: hide(d >= 0)))
    j, i = np.arange(128)[:, None], np.arange(128)[None, :]
    lv = [(j == i)]
    for s in (1, 2, 4, 8, 16, 32):
        lv.append((j // (2 * s) == i // (2 * s)) & ((j // s) % 2 == 0) & ((i // s) % 2 == 1))
    put("levels", np.concatenate(lv, axis=1))
    put("block", (j // 32 == np.arange(256)[None, :] // 64))
    second = np.concatenate(parts, axis=1)[:, keep:]
    out = np.zeros((128, first.shape[1] + second.shape[1]), np.float32)
    out[:, 0:first.shape[1]] = first
    out[:, first.shape[1]:] = second
    return out, keep, first.shape[1], second.shape[1]


CONST_ARRAY, KEEP, FIRST, SECOND = _consts()


class Queues:

    def __init__(self, nc, ctx):
        self.nc, self.ctx = nc, ctx
        self.q = {e: [] for e in ("pe", "act", "dve", "pool", "sp")}
        self.sem = {e: ctx.enter_context(nc.semaphore("s_" + e)) for e in ("pe", "act", "dve", "pool")}
        self.n = dict.fromkeys(self.q, 0)
        self.seen = {e: {} for e in self.q}
        self.past = []

    def waits(self, e, after):
        for a in after:
            if a is None:
                continue
            if isinstance(a, list):
                self.waits(e, a)
                continue
            s, v = a
            if self.seen[e].get(id(s), 0) < v:
                self.seen[e][id(s)] = v
                self.q[e].append(("wait", s, v))

    def op(self, e, fn, *after, sig=True):
        self.waits(e, after)
        if not sig:
            self.q[e].append(("op", fn, None, 0))
            return None
        self.n[e] += 1
        self.q[e].append(("op", fn, self.sem[e], 1))
        return (self.sem[e], self.n[e])

    def dma(self, e, out, src, sem, value, *after, **k):
        self.waits(e, after)
        self.q[e].append(("op", lambda g, o=out, s=src, k=k: g.dma_start(o, s, **k), sem, 16))
        return (sem, value)

    def last(self, e):
        return (self.sem[e], self.n[e]) if self.n[e] else None

    def fence(self, t=None):
        if t is None:
            t = [self.last(e) for e in ("pe", "act", "dve", "pool")]
        for e in ("act", "dve", "pool"):
            self.waits(e, t)
        self.past = t

    def emit(self, block):
        for e, deco in (("pe", block.tensor), ("act", block.scalar), ("dve", block.vector),
                        ("pool", block.gpsimd), ("sp", block.sync)):
            items = self.q[e]

            def run(eng, items=items):
                for it in items:
                    if it[0] == "wait":
                        eng.wait_ge(it[1], it[2])
                    else:
                        ins = it[1](eng)
                        if it[2] is not None:
                            ins.then_inc(it[2], it[3])
            deco(run)


def build(nc, A, out):
    ctx = ExitStack()
    with ctx:
        Q = Queues(nc, ctx)
        op = Q.op

        def sb(name, shape, dt=F32, c=ctx):
            return c.enter_context(nc.sbuf_tensor(name, shape, dt))

        class Region:

            def __init__(self, t, lo, hi):
                self.t, self.at, self.hi = t, lo, hi

            def __call__(self, name, shape, c=None):
                n = int(np.prod(shape[1:]))
                v = self.t[0:shape[0], self.at:self.at + n]
                self.at += n
                assert self.at <= self.hi, (name, self.at, self.hi)
                if len(shape) == 3:
                    v = v.rearrange("p (a b) -> p a b", a=shape[1])
                if len(shape) == 4:
                    v = v.rearrange("p (a b c) -> p a b c", a=shape[1], b=shape[2])
                return v

        def sem(name):
            return ctx.enter_context(nc.semaphore(name))

        PS = ctx.enter_context(nc.psum_tensor("ps", [128, 8, 512], F32))
        banks = [PS[:, i, :] for i in range(8)]
        free = [(i, None) for i in range(8)]

        def bank():
            i, t = free.pop(0)
            return i, banks[i], t

        def pair(bb):
            i = bb[0][0]
            return PS[:, i:i + 2, :]

        def bank2():
            at = {i: n for n, (i, _) in enumerate(free)}
            i = min((i for i in at if i % 2 == 0 and i + 1 in at), key=lambda i: max(at[i], at[i + 1]))
            bb = [free[at[j]] for j in (i, i + 1)]
            for x in bb:
                free.remove(x)
            return [(j, banks[j], t) for j, t in bb]

        def release(i, *t):
            free.append((i, list(t)))

        def mm(o, l, r, start, stop, *after, sig=None):
            return op("pe", lambda e: e.matmul(o, l, r, start=start, stop=stop), *after,
                      sig=stop if sig is None else sig)

        def mm3(o, lh, ll, rh, rl, start, stop, *after, sig=False):
            mm(o, lh, rh, start, False, *after, sig=False)
            mm(o, lh, rl, False, False, sig=False)
            return mm(o, ll, rh, False, stop, sig=sig)

        def tp(o, i, idn, *after, sig=True):
            return op("pe", lambda e: e.transpose(o, i, idn), *after, sig=sig)

        def act(o, i, f, *after, **k):
            return op("act", lambda e: e.activation(o, i, f, **k), *after)

        def cp(o, i, *after, e="dve"):
            if e == "act":
                return act(o, i, ACT.Copy, *after)
            return op(e, lambda g: g.tensor_copy(o, i), *after)

        def tt(o, a, b, f, *after, e="dve"):
            return op(e, lambda g: g.tensor_tensor(o, a, b, f), *after)

        def ts(o, a, s1, s2, f1, f2, *after, e="dve"):
            if f2 is None:
                return op(e, lambda g: g.tensor_scalar(o, a, s1, None, f1), *after)
            return op(e, lambda g: g.tensor_scalar(o, a, s1, s2, f1, f2), *after)

        def stt(o, a, s, b, f1, f2, *after):
            return op("dve", lambda g: g.scalar_tensor_tensor(out=o, in0=a, scalar=s, in1=b, op0=f1, op1=f2), *after)

        def ttr(o, a, b, scale, init, f1, f2, acc, *after):
            return op("dve", lambda g: g.tensor_tensor_reduce(out=o, in0=a, in1=b, scale=scale, scalar=init,
                                                              op0=f1, op1=f2, accum_out=acc), *after)

        def red(o, a, f, *after):
            return op("dve", lambda g: g.tensor_reduce(o, a, AX, f), *after)

        def rcp(o, a, *after):
            return op("dve", lambda g: g.reciprocal(o, a), *after)

        def memset(o, v, *after, e="pool"):
            return op(e, lambda g: g.memset(o, v), *after)

        xs = sb("xs", [128, 2, D])
        hTh = sb("hTh", [128, KD, S], F32R)
        hTl = sb("hTl", [128, KD, S], F32R)
        stage = [sb(f"stage{i}", [128, CH]) for i in range(NS)]
        whi = [sb(f"whi{i}", [128, CH], F32R) for i in range(NH)]
        wlo = [sb(f"wlo{i}", [128, CH], F32R) for i in range(NH)]
        NCC = max(FIRST, KEEP + SECOND)
        cst = sb("cst", [128, NCC])
        st8 = sb("st8", [128, 16])
        phalf = sb("phalf", [128, 32])
        gcol = sb("gcol", [128, 8, 11])
        junk = sb("junk", [128, D], mybir.dt.bfloat16)
        R2 = sb("R2", [128, 2 * S])
        dg = sb("dg", [128, 2, 128])

        def C(name, lo=0, n=None):
            o, w = CONSTS[name]
            return cst[:, o + lo:o + (w if n is None else lo + n)]

        ident = C("ident")
        s_x, s_c, s_o = [sem("s_x0"), sem("s_x1")], sem("s_c"), sem("s_o")
        s_st = [sem(f"s_st{i}") for i in range(NS)]
        s_g = sem("s_g")
        s_par = sem("s_par")

        s_k = sem("s_k")
        xv = A["x"][0].rearrange("(t p) d -> p t d", p=128)
        t_x = {}
        for n in range(2):
            w = Q.dma("sp", xs[:, :, n * 512:n * 512 + 512], xv[:, :, n * 512:n * 512 + 512], s_x[n], 16)
            t_x[0, n] = t_x[1, n] = w
            if n == 0:
                t_c = Q.dma("sp", cst[:, 0:KEEP], A["consts"][:, 0:KEEP], s_k, 16)
        t_ph = memset(phalf[:, :], -0.5)
        npar = [0]

        def par(o, src, *after):
            npar[0] += 16
            return Q.dma("sp", o, src, s_par, npar[0], Q.past, *after, allow_slow_non_contiguous=True)

        plan = []

        def view(c, shape):
            n = int(np.prod(shape))
            v = c[:, 0:n]
            if len(shape) == 2:
                return v.rearrange("p (a b) -> p a b", a=shape[0])
            return v

        def plan_cols(w, k0, nk, c0, nc_):
            src = w[k0 * 128:(k0 + nk) * 128, c0:c0 + nc_].rearrange("(k p) n -> p k n", p=128)
            plan.append(([(0, src, (nk, nc_))], nk * nc_))

        def plan_rows(w, rows):
            plan.append(([(i * 1024, w[r:r + 128, :], (1, 1024)) for i, r in enumerate(rows)], 1024 * len(rows)))

        def plan_up(wg, wu, F):
            c = 0
            while c < F:
                if F - c >= 256:
                    plan_cols(wg, 0, 8, c, 256)
                    plan_cols(wu, 0, 8, c, 256)
                    c += 256
                    continue
                assert F - c == 192

                def cols(w, k0, k1, a, b):
                    return w[k0 * 128:k1 * 128, a:b].rearrange("(k p) n -> p k n", p=128)

                for i, w in enumerate((wg, wu)):
                    k0 = 4 * i
                    plan.append(([(0, cols(w, 0, 8, c, c + 128), (8, 128)),
                                  (1024, cols(wg, k0, k0 + 4, c + 128, F), (4, 128), 0),
                                  (1024, cols(wu, k0, k0 + 4, c + 128, F), (4, 128), 64)], 1536))
                c = F

        def row_starts(F):
            r = [i * 128 for i in range(F // 128)]
            if F % 128:
                r.append(F - 128)
            return r

        def plan_down(w, F):
            r = row_starts(F)
            for i in range(0, len(r), 2):
                plan_rows(w, r[i:i + 2])

        def plan_x(w, c0, n):
            if n <= 256:
                plan_cols(w, 0, 8, c0, n)
            else:
                plan_cols(w, 0, 4, c0, n)
                plan_cols(w, 4, 4, c0, n)

        ffns = []
        for l in range(2):
            for s in range(2):
                ffns.append((A["ffn_w_gate"][l, s], A["ffn_w_up"][l, s], A["ffn_w_down"][l, s], F1))
        for l in range(2):
            ffns.append((A["w_ffn_gate_2"][l], A["w_ffn_up_2"][l], A["w_ffn_down_2"][l], F2))

        def plan_ffn(i):
            wg, wu, wd, F = ffns[i]
            plan_up(wg, wu, F)
            plan_down(wd, F)

        ev, od = A["ev_w_in"][0], A["od_w_in"][0]
        X2 = [(1184, 512, 416), (1696, 512, 928), (2208, 440, 1440), (0, 416, 0)]

        FILL = [(1, False), (3, False), (1, True), (2, False), (0, False), (3, True), (2, True), (0, True)]

        def plan_even():
            for c in (0, 256):
                plan_cols(ev, 0, 8, c, 256)
                plan_cols(ev, 0, 8, 512 + c, 256)
                if c == 0:
                    plan_x(ev, 1024, 512)
                    plan_x(ev, 1536, 256)
            for row_ in (512, 768, 0, 256):
                plan_rows(A["ev_w_out"][0], [row_, row_ + 128])

        def plan_odd():
            for c in (0, 512, 1024):
                plan_x(od, c, 512)
            for c in (1536, 1792):
                plan_cols(od, 0, 8, c, 256)
            for row_ in (512, 768, 0, 256):
                plan_rows(A["od_w_out"][0], [row_, row_ + 128])

        def plan_mixer2(l):
            w2 = A["w_in_2"][l]
            for c, n, _ in X2:
                plan_x(w2, c, n)
            for c in (416, 672, 928):
                plan_cols(w2, 0, 8, c, 256)
            for n, merge in FILL:
                if merge:
                    plan_rows(A["w_branch_2"][l, n], [0, 128])
                else:
                    for c in range(4):
                        plan_cols(w2, 0, 8, 2648 + 1024 * n + 256 * c, 256)
            plan_down(A["w_out_2"][l], 1024)

        plans = [lambda: plan_ffn(0), plan_even, lambda: plan_ffn(1), lambda: plan_ffn(2), plan_odd,
                 lambda: plan_ffn(3), lambda: plan_mixer2(0), lambda: plan_ffn(4), lambda: plan_mixer2(1),
                 lambda: plan_ffn(5)]
        for p in plans:
            p()

        stage_free = [None] * NS
        stage_ready = {}
        half_free = [None] * NH
        split_done = {}
        nxt = {"dma": 0, "split": 0, "use": 0}

        def issue_dma():
            i = nxt["dma"]
            if i >= len(plan):
                return
            nxt["dma"] += 1
            s = i % NS
            parts, n = plan[i]
            k = stage_count[s]
            for off, src, shape, *at in parts:
                k += 1
                dst = stage[s][:, off:off + shape[0] * shape[1]]
                if len(src.shape) == 3:
                    dst = dst.rearrange("p (a b) -> p a b", a=shape[0])
                for c in at:
                    dst = dst[:, :, c:c + src.shape[2]]
                t = Q.dma("sp", dst, src, s_st[s], 16 * k, stage_free[s])
            stage_count[s] = k
            stage_ready[i] = t

        stage_count = [0] * NS

        def issue_split():
            i = nxt["split"]
            if i >= len(plan):
                return
            nxt["split"] += 1
            s, h = i % NS, i % NH
            n = plan[i][1]
            t2 = []
            for a, b, e in ((0, n // 2, lo_engine[0]), (n // 2, n, "dve")):
                t1 = act(whi[h][:, a:b], stage[s][:, a:b], ACT.Copy, stage_ready[i], half_free[h])
                t2.append(tt(wlo[h][:, a:b], stage[s][:, a:b], whi[h][:, a:b].bitcast(F32), ALU.subtract, t1,
                             half_free[h], e=e))
            stage_free[s] = t2
            split_done[i] = t2
            issue_dma()

        def take():
            i = nxt["use"]
            nxt["use"] += 1
            return i, whi[i % NH], wlo[i % NH], split_done[i]

        later = []
        lo_engine = ["dve"]
        behind = []

        def catch_up():
            while behind:
                b = behind.pop(0)
                if b is None:
                    issue_split()
                else:
                    used(*b)

        def used(i, t):
            half_free[i % NH] = t
            issue_split()
            for g in list(later):
                if next(g, "end") == "end":
                    later.remove(g)

        def flush():
            for g in list(later):
                for _ in g:
                    pass
                later.remove(g)

        issue_dma()
        rope = sb("rope", [128, 2, 2, 16])
        cr = ctx.enter_context(ExitStack())
        grow = sb("grow", [10, D], c=cr)
        Q.dma("act", grow[0:6, :], A["norm_g"].rearrange("l j n -> (l j) n"), s_g, 16)
        Q.dma("act", grow[6:8, :], A["attn_norm_g_2"], s_g, 32)
        t_g = Q.dma("act", grow[8:10, :], A["ffn_norm_g_2"], s_g, 48)
        issue_dma()
        t_c1 = Q.dma("sp", cst[:, KEEP:FIRST], A["consts"][:, KEEP:FIRST], s_c, 16)
        for _ in range(NS - 2):
            issue_dma()

        def split_T(ps, dh, dl, t, scale=1.0):
            a = act(dh, ps, ACT.Copy, t, scale=scale)
            if scale == 1.0:
                return tt(dl, ps, dh.bitcast(F32), ALU.subtract, a)
            return stt(dl, ps, scale, dh.bitcast(F32), ALU.mult, ALU.subtract, a)

        def transposed(src, nk, dh, dl, after):
            toks = []
            for k0 in range(0, nk, 2):
                b, ps, f = bank()
                m = min(2, nk - k0)
                for j in range(m):
                    for t in range(2):
                        c = (2 * j + t) * 128
                        w = tp(ps[:, c:c + 128], src(k0 + j, t), ident, f, after(k0 + j, t), t_c,
                               sig=(j == m - 1 and t == 1))
                o = slice(k0, k0 + m)
                z = split_T(ps[:, 0:m * 256], dh[:, o, :].rearrange("p k s -> p (k s)"),
                            dl[:, o, :].rearrange("p k s -> p (k s)"), w)
                release(b, z)
                toks.append(z)
            return toks

        def power(o, a, n, *after):
            return tt(o, a, phalf[:, 0:n], ALU.pow, *after, t_ph, e="pool")

        def rms_col(tin):
            a = Q.last("act")
            for t in range(2):
                a = act(junk[:, :], xs[:, t, :], ACT.Square, tin[t, 0], tin[t, 1], a, accum_out=st8[:, t:t + 1])
            b = ts(st8[:, 2:4], st8[:, 0:2], 1.0 / D, EPS, ALU.mult, ALU.add, a)
            return power(st8[:, 4:6], st8[:, 2:4], 2, b)

        def norm_T(i, tin):
            hr = []
            for k in range(KD):
                b, ps, f = bank()
                for t in range(2):
                    w = tp(ps[:, t * 128:t * 128 + 128], xs[:, t, k * 128:k * 128 + 128], ident, f,
                           tin[t, k // 4], t_c, sig=(t == 1))
                g = gcol[:, k, i:i + 1]
                a = act(hTh[:, k, :], ps[:, 0:256], ACT.Copy, w, t_gc, scale=g)
                z = stt(hTl[:, k, :], ps[:, 0:256], g, hTh[:, k, :].bitcast(F32), ALU.mult, ALU.subtract, a)
                release(b, z)
                hr.append(z)
            catch_up()
            tcol = rms_col(tin)
            zr = []

            def diag():
                for t in range(2):
                    zr[:] = [ts(dg[:, t, :], ident, st8[:, 4 + t:5 + t], 512.0, ALU.mult, ALU.mult, tcol, zr)]

            def row():
                if not zr:
                    diag()
                z = zr
                b, ps, f = bank()
                for t in range(2):
                    w = mm(ps[:, t * 128:t * 128 + 128], C("ones"), dg[:, t, :], True, True, f, z)
                z = cp(R2[:, :].rearrange("p (a s) -> p a s", a=2), ps[:, 0:256].unsqueeze(1).broadcast_to([128, 2, 256]), w)
                release(b, z)
                return z

            row.diag = diag
            return hr, tcol, row

        R22 = R2[:, :].rearrange("p (a s) -> p a s", a=2)
        R24 = R2[:, :].unsqueeze(1).broadcast_to([128, 2, 2 * S])

        def two(x):
            return x.rearrange("p (a s) -> p a s", a=2)

        def up_tile(ps, c0, wh, wl, w_cols, col, sd, hready, f):
            wvh, wvl = view(wh, (8, w_cols)), view(wl, (8, w_cols))
            for k in range(8):
                t = mm3(ps[:, c0:c0 + 256], wvh[:, k, col:col + 128], wvl[:, k, col:col + 128],
                        hTh[:, k, :], hTl[:, k, :], k == 0, k == 7, f, sd, hready[k], sig=(k == 7))
            return t

        def x_cols(n, hready):
            bb = [bank(), bank()]
            nk = 8 if n <= 256 else 4
            for c in range(8 // nk):
                i, wh, wl, sd = take()
                vh, vl = view(wh, (nk, n)), view(wl, (nk, n))
                toks = []
                for t in range(2):
                    sl = slice(t * 128, t * 128 + 128)
                    for kk in range(nk):
                        k = c * nk + kk
                        tk = mm3(bb[t][1][:, 0:n], hTh[:, k, sl], hTl[:, k, sl], vh[:, kk, :], vl[:, kk, :],
                                 k == 0, k == 7, bb[t][2], sd, hready[k], sig=(kk == nk - 1))
                    toks.append(tk)
                    if t == 1:
                        behind.append((i, tk))
                    yield
            return [(bb[t][0], bb[t][1], toks[t]) for t in range(2)]

        def by_token(o, ps, t, *after, e="act"):
            if e == "act":
                return act(o, ps, ACT.Copy, *after, scale=st8[:, 4 + t:5 + t])
            return ts(o, ps, st8[:, 4 + t:5 + t], None, ALU.mult, None, *after)

        def down(parts, coef):
            run(down_g(parts, coef, toks := {}))
            return toks

        def down_g(parts, coef, toks):
            bb = [[bank() for n in range(2)] for t in range(2)]
            nk = len(parts)
            for k0 in range(0, nk, 2):
                while None in parts[k0:k0 + 2]:
                    yield
                i, wh, wl, sd = take()
                for n in range(2):
                    for t in range(2):
                        b, ps, f = bb[t][n]
                        for k in range(k0, min(nk, k0 + 2)):
                            h, lo, sl, tk = parts[k]
                            c = (k - k0) * 1024 + n * 512
                            w = mm3(ps[:, :], h[sl, t * 128:t * 128 + 128], lo[sl, t * 128:t * 128 + 128],
                                    wh[sl, c:c + 512], wl[sl, c:c + 512], k == 0, k == nk - 1,
                                    f, sd, tk, sig=(k == nk - 1 or (t == 1 and n == 1 and k % 2 == 1)))
                        if k == nk - 1:
                            o = xs[:, t, n * 512:(n + 1) * 512]
                            if coef == 1.0:
                                z = tt(o, ps[:, :], o, ALU.add, w)
                            else:
                                z = stt(o, ps[:, :], coef, o, ALU.mult, ALU.add, w)
                            release(b, z)
                            toks[t, n] = z
                        if t == 0 or n == 0:
                            yield
                if k0 + 2 < nk:
                    behind.append((i, w))
                    yield
            behind.append((i, w))

        everyrow = slice(0, 128)

        def ffn(i, gl, tin, coef):
            F = ffns[i][3]
            nf = len(row_starts(F))
            with ExitStack() as c:
                fh = sb(f"fh{i}", [128, 22, S], F32R, c)
                fl = sb(f"fl{i}", [128, 22, S], F32R, c)
                sg = [sb(f"sg{i}_{j}", [128, 2, 2 * S], c=c) for j in range(2)]
                hr, tcol, row = norm_T(gl, tin)
                tR = None
                parts = [None] * nf
                sg_free = [None, None]

                def post(bb, f, w, s, k):
                    m = tt(s[:, :, :], pair(bb), R24, ALU.mult, w, sg_free[k], tR)
                    release(bb[0][0], m)
                    release(bb[1][0], m)
                    a = act(s[:, :, 0:256], s[:, :, 0:256], ACT.Silu, m)
                    yield
                    m = tt(s[:, :, 0:256], s[:, :, 0:256], s[:, :, 256:512], ALU.mult, a)
                    h = act(fh[:, f:f + 2, :], s[:, :, 0:256], ACT.Copy, m)
                    lo = tt(fl[:, f:f + 2, :], s[:, :, 0:256], fh[:, f:f + 2, :].bitcast(F32), ALU.subtract, h)
                    sg_free[k] = lo
                    for j in range(2):
                        parts[f + j] = (fh[:, f + j, :], fl[:, f + j, :], everyrow, lo)

                def post_last(bb, f, w, s, k):
                    top, low = slice(0, 64), slice(64, 128)
                    m = tt(s[:, 0, :], bb[0][1], R2[:, :], ALU.mult, w, sg_free[k], tR)
                    m = tt(s[:, 1, 0:256], bb[1][1][:, 0:256], R2[:, 0:256], ALU.mult, m)
                    release(bb[0][0], m)
                    release(bb[1][0], m)
                    a = act(s[:, 0, 0:256], s[:, 0, 0:256], ACT.Silu, m)
                    a = act(s[low, 1, 256:512], s[top, 1, 0:256], ACT.Silu, a)
                    yield
                    for j, sl in ((0, everyrow), (1, low)):
                        m = tt(s[sl, j, 0:256], s[sl, j, 0:256], s[sl, j, 256:512], ALU.mult, a, m)
                        h = act(fh[sl, f + j, :], s[sl, j, 0:256], ACT.Copy, m)
                        lo = tt(fl[sl, f + j, :], s[sl, j, 0:256], fh[sl, f + j, :].bitcast(F32), ALU.subtract, h)
                        parts[f + j] = (fh[:, f + j, :], fl[:, f + j, :], sl, lo)
                    sg_free[k] = lo

                f = 0
                col = 0
                while col < F:
                    n = 256
                    bb = bank2()
                    k = (f // 2) % 2
                    if F - col < 256:
                        for c in range(2):
                            i0, wh, wl, sd = take()
                            up_tile(bb[0][1], 256 * c, wh, wl, 128, 0, sd, hr, bb[0][2])
                            vh, vl = [view(x[:, 1024:1536], (4, 128)) for x in (wh, wl)]
                            for kk in range(4):
                                k8 = 4 * c + kk
                                tu = mm3(bb[1][1][:, 0:256], vh[:, kk, :], vl[:, kk, :], hTh[:, k8, :], hTl[:, k8, :],
                                         k8 == 0, k8 == 7, bb[1][2], sd, hr[k8], sig=(kk == 3))
                            if c == 0:
                                used(i0, tu)
                        later.append(post_last(bb, f, tu, sg[k], k))
                        used(i0, tu)
                        f += 2
                        break
                    i0, wh, wl, sd = take()
                    for j in range(2):
                        tg = up_tile(bb[j][1], 0, wh, wl, n, 128 * j, sd, hr, bb[j][2])
                    used(i0, tg)
                    if tR is None:
                        row.diag()
                    i0, wh, wl, sd = take()
                    for j in range(2):
                        tu = up_tile(bb[j][1], 256, wh, wl, n, 128 * j, sd, hr, None)
                    if tR is None:
                        tR = row()
                    later.append(post(bb, f, tu, sg[k], k))
                    used(i0, tu)
                    f += 2
                    col += n
                assert f == nf
                r = down(parts, coef)
            return r

        def run(*gens):
            gens = [g for g in gens]
            while gens:
                for g in list(gens):
                    try:
                        next(g)
                    except StopIteration:
                        gens.remove(g)
                if gens:
                    catch_up()

        def heads_T(dst, d, H, src, after, scale=None, e="act"):
            toks = []
            for h0 in range(0, H, 2):
                b, ps, f = bank()
                m = min(2, H - h0)
                for j in range(m):
                    for t in range(2):
                        c = (2 * j + t) * 128
                        w = tp(ps[0:d, c:c + 128], src(h0 + j, t), ident, f, after, t_c,
                               sig=(j == m - 1 and t == 1))
                o = dst[:, h0:h0 + m, :].rearrange("p h s -> p (h s)")
                if e == "act":
                    k = {} if scale is None else {"scale": scale}
                    z = act(o, ps[0:d, 0:m * 256], ACT.Copy, w, **k)
                elif scale is None:
                    z = cp(o, ps[0:d, 0:m * 256], w)
                else:
                    z = ts(o, ps[0:d, 0:m * 256], scale, None, ALU.mult, None, w)
                release(b, z)
                toks.append(z)
            return toks

        def attention(name, al, H, qT, kT, vN, mask, scale, ready, dst, sink=None, mult=None, mready=None,
                      apart=False):
            sm = [al(f"{name}_sm{i}", [128, 2, 256]) for i in range(3)]
            pt = [al(f"{name}_pt{i}", [128, 512]) for i in range(2)]
            mx = al(f"{name}_mx", [128, 4, 16])
            sm_free, pt_free = [None] * 3, [None] * 2
            done, obank = [None, None], {}

            def group(t, h0, turn):
                nk = 128 * (t + 1)
                i, ip = turn % 3, turn % 2
                b, ps, f = bank()
                w = None
                for j in range(2):
                    w = mm(ps[:, j * 256:j * 256 + nk], qT(h0 + j)[:, t * 128:t * 128 + 128],
                           kT(h0 + j)[:, 0:nk], True, True, f, ready, w if apart else None)
                c0 = t * 8 + h0
                for j in range(2):
                    z = ttr(sm[i][:, j, 0:nk], ps[:, j * 256:j * 256 + nk], mask(t), scale, -3e38, ALU.add,
                            ALU.max, mx[:, 0, c0 + j:c0 + j + 1], w, sm_free[i], t_c1, ready, mready)
                release(b, z)
                if sink is not None:
                    z = tt(mx[:, 0, c0:c0 + 2], mx[:, 0, c0:c0 + 2], sink[:, h0:h0 + 2], ALU.max, z)
                z = ts(mx[:, 1, c0:c0 + 2], mx[:, 0, c0:c0 + 2], -1.0, None, ALU.mult, None, z)
                yield
                for j in range(2):
                    k = {} if mult is not None else {"accum_out": mx[:, 2, c0 + j:c0 + j + 1]}
                    a = act(sm[i][:, j, 0:nk], sm[i][:, j, 0:nk], ACT.Exp, z, bias=mx[:, 1, c0 + j:c0 + j + 1], **k)
                if mult is not None:
                    for j in range(2):
                        a = ttr(sm[i][:, j, 0:nk], sm[i][:, j, 0:nk], mult(t), 1.0, 0.0, ALU.mult, ALU.add,
                                mx[:, 2, c0 + j:c0 + j + 1], a)
                yield
                b, ps, f = bank()
                for j in range(2):
                    for kt in range(t + 1):
                        o = (j * (t + 1) + kt) * 128
                        w = tp(ps[:, o:o + 128], sm[i][:, j, kt * 128:kt * 128 + 128], ident, f, a, t_c,
                               sig=(j == 1 and kt == t))
                sm_free[i] = w
                z = cp(pt[ip][:, 0:256 * (t + 1)], ps[:, 0:256 * (t + 1)], w, pt_free[ip], e="act")
                release(b, z)
                yield
                if t not in obank:
                    obank[t] = bank()
                ob, ops_, of = obank[t]
                for j in range(2):
                    for kt in range(t + 1):
                        o = (j * (t + 1) + kt) * 128
                        w = mm(ops_[:, (h0 + j) * 64:(h0 + j) * 64 + 64], pt[ip][:, o:o + 128], vN(kt, h0 + j),
                               kt == 0, kt == t, z, of, sig=(j == 1 and kt == t))
                pt_free[ip] = w
                if h0 != H - 2:
                    return
                c0 = t * 8
                l = mx[:, 2, c0:c0 + H]
                tail = a
                if sink is not None:
                    z = tt(mx[:, 3, c0:c0 + H], sink[:, 0:H], mx[:, 1, c0:c0 + H], ALU.add, a)
                    z = act(mx[:, 3, c0:c0 + H], mx[:, 3, c0:c0 + H], ACT.Exp, z)
                    tail = tt(l, l, mx[:, 3, c0:c0 + H], ALU.add, z)
                z = rcp(mx[:, 3, c0:c0 + H], l, tail)
                z = tt(dst[:, t, :].rearrange("p (h e) -> p h e", h=H),
                       ops_[:, 0:H * 64].rearrange("p (h e) -> p h e", h=H),
                       mx[:, 3, c0:c0 + H].unsqueeze(2).broadcast_to([128, H, 64]), ALU.mult, z, w)
                release(ob, z)
                done[t] = z

            todo = [(t, h0) for t in range(2) for h0 in range(0, H, 2)]
            active, turn = [], 0
            while todo or active:
                for g in list(active):
                    if next(g, "end") == "end":
                        active.remove(g)
                if todo:
                    g = group(*todo.pop(0), turn)
                    turn += 1
                    next(g)
                    active.append(g)
                yield
            return done

        def head_norm(name, al, src, H, d, after, sq=None):
            if sq is None:
                sq = al(name + "_sq", [128, 2, H * d])
            r = al(name + "_r", [128, 2, H])
            a = act(sq[:, :, :], src, ACT.Square, after)
            z = red(r[:, :, :], sq[:, :, :].rearrange("p t (h d) -> p t h d", h=H), ALU.add, a)
            z = ts(r[:, :, :], r[:, :, :], 1.0 / d, EPS, ALU.mult, ALU.add, z)
            rf = r[:, :, :].rearrange("p t h -> p (t h)")
            return r, power(rf, rf, 2 * H, z)

        def even_mixer(gl, tin):
            with ExitStack() as c:
                Q.fence()
                hr, tcol, row = norm_T(gl, tin)
                def sbc(name, shape):
                    return sb(name, shape, c=c)

                u = sb("ev_u", [128, 4, PAD + S], c=c)
                acc = sb("ev_acc", [128, 4, S], c=c)
                acc2 = sb("ev_acc2", [128, 4, S], c=c)
                tm = sb("ev_tm", [128, 4, S], c=c)
                sq = sb("ev_sqc", [128, 4, S], c=c)
                rs = sb("ev_rs", [128, S], c=c)
                th = [sb(f"ev_th{i}", [128, 2 * S], c=c) for i in range(2)]
                vr = sb("ev_vr", [128, 4], c=c)
                qkv = sb("ev_qkv", [128, 2, 768], c=c)
                qT = sb("ev_qT", [64, 8, S], c=c)
                kT = sb("ev_kT", [64, 2, S], c=c)
                o = sb("ev_o", [128, 2, 512], c=c)
                mh = sb("ev_mh", [128, 8, S], F32R, c)
                ml = sb("ev_ml", [128, 8, S], F32R, c)
                cwr = sb("ev_cwr", [34, 512], c=c)
                cw = sb("ev_cw", [128, 4, 34], c=c)
                cb = sb("ev_cb", [128, 3, 4], c=c)
                qg = sb("ev_qg", [64, 2], c=c)
                sk = sb("ev_sk", [128, 8], c=c)
                z0 = memset(u[:, :, 0:PAD], 0.0)
                par(cwr[0:31, :], A["ev_conv_w"][0])
                par(cwr[31:32, :], A["ev_conv_b"])
                par(cwr[32:33, :], A["ev_ln_g"])
                par(cwr[33:34, :], A["ev_ln_b"])
                par(qg[:, 0:1], A["ev_q_norm_g"][0].rearrange("(p a) -> p a", a=1))
                par(qg[:, 1:2], A["ev_k_norm_g"][0].rearrange("(p a) -> p a", a=1))
                tpar = par(sk[:, :], A["ev_sinks"].broadcast_to([128, 8]))
                res = {}
                parts = [None] * 8
                du = [None] * 4
                tq = []

                def products():
                    tR = None
                    for j0 in (0, 2):
                        bb = [bank(), bank()]
                        for c0 in (0, 256):
                            i0, wh, wl, sd = take()
                            tl = []
                            for j in range(2):
                                tl.append(up_tile(bb[j][1], c0, wh, wl, 256, j * 128, sd, hr, bb[j][2]))
                                if j:
                                    behind.append((i0, tl[1]))
                                    if c0 == 0 and j0 == 0:
                                        row.diag()
                                    elif tR is None:
                                        tR = row()
                                        conv_weights()
                                yield
                        for j in range(2):
                            z = tt(two(th[j][:, :]), two(bb[j][1][:, :]), R22, ALU.mult, tl[j], du[j], tR)
                            release(bb[j][0], z)
                            a = act(th[j][:, 256:512], th[j][:, 256:512], ACT.Tanh, z, scale=0.5)
                            du[j0 + j] = stt(u[:, j0 + j, PAD:], th[j][:, 256:512], 1.0, th[j][:, 0:256], ALU.add,
                                             ALU.mult, a)
                        if j0:
                            break
                        for c0, n in ((0, 512), (512, 256)):
                            q0 = yield from x_cols(n, hr)
                            for t in range(2):
                                z = by_token(qkv[:, t, c0:c0 + n], q0[t][1][:, 0:n], t, q0[t][2], tcol)
                                release(q0[t][0], z)
                                tq.append(z)

                def conv_weights():
                    b, ps, f = bank()
                    for j in range(4):
                        w = tp(ps[:, j * 34:(j + 1) * 34], cwr[:, j * 128:(j + 1) * 128], ident[0:34, 0:34], f, tpar,
                               t_c)
                    z = cp(cw[:, :, :].rearrange("p a b -> p (a b)"), ps[:, 0:136], w)
                    release(b, z)
                    res["cw"] = z
                    res["ch"] = ts(cw[:, :, 0:31], cw[:, :, 0:31], 0.5, None, ALU.mult, None, z)

                def conv():
                    cur, cu2 = [None] * 4, [None] * 4
                    tm_free = [None] * 4
                    turn = itertools.count()

                    def side_tap(k, j):
                        if k is None:
                            return
                        src = u[:, j, PAD - (CONV_W - 1) + k:][:, 0:S]
                        if k == 0:
                            cu2[j] = act(acc2[:, j, :], src, ACT.Copy, du[j], res["ch"], z0, scale=cw[:, j, 0:1])
                            return
                        m = next(turn) % 4
                        a = act(tm[:, m, :], src, ACT.Copy, du[j], tm_free[m], scale=cw[:, j, k:k + 1])
                        cu2[j] = tm_free[m] = tt(acc2[:, j, :], acc2[:, j, :], tm[:, m, :], ALU.add, a, cu2[j],
                                                 e="pool")

                    for jj in ((0, 1), (2, 3)):
                        while du[jj[1]] is None:
                            yield
                        side = iter([(k, j) for k in range(SIDE) for j in jj])
                        for k in range(SIDE, CONV_W):
                            for j in jj:
                                src = u[:, j, PAD - (CONV_W - 1) + k:][:, 0:S]
                                if k == SIDE:
                                    cur[j] = ts(acc[:, j, :], src, cw[:, j, k:k + 1], cw[:, j, 31:32], ALU.mult,
                                                ALU.add, du[j], res["ch"], z0)
                                else:
                                    cur[j] = stt(acc[:, j, :], src, cw[:, j, k:k + 1], acc[:, j, :], ALU.mult,
                                                 ALU.add, cur[j])
                            for _ in range(SIDE_RATE):
                                side_tap(*next(side, (None, None)))
                            if (k - SIDE) % 2:
                                yield
                        assert next(side, None) is None
                        yield
                        for j in jj:
                            cur[j] = tt(acc[:, j, :], acc[:, j, :], acc2[:, j, :], ALU.add, cur[j], cu2[j])
                    res["conv"] = cur

                def layer_norm():
                    cur = res["conv"]
                    b, ps, f = bank()
                    for j in range(4):
                        w = mm(ps[:, 0:256], C("ones"), acc[:, j, :], j == 0, j == 3, f, cur[j])
                    yield
                    z = tt(acc[:, :, :], acc[:, :, :], ps[:, 0:256].unsqueeze(1).broadcast_to([128, 4, 256]),
                           ALU.subtract, w)
                    release(b, z)
                    a = act(sq[:, :, :], acc[:, :, :], ACT.Square, z)
                    yield
                    b, ps, f = bank()
                    for t in range(2):
                        for j in range(4):
                            w = mm(ps[:, t:t + 1], sq[:, j, t * 128:t * 128 + 128], C("ones", 0, 1), j == 0, j == 3,
                                   f, a)
                    z2 = ts(vr[:, 0:2], ps[:, 0:2], EPS, None, ALU.add, None, w)
                    release(b, z2)
                    z2 = power(vr[:, 2:4], vr[:, 0:2], 2, z2)
                    for t in range(2):
                        z2 = ts(dg[:, t, :], ident, vr[:, 2 + t:3 + t], 512.0, ALU.mult, ALU.mult, z2)
                    b, ps, f = bank()
                    for t in range(2):
                        w = mm(ps[:, t * 128:t * 128 + 128], C("ones"), dg[:, t, :], True, True, f, z2)
                    z2 = cp(rs[:, :], ps[:, 0:256], w)
                    release(b, z2)
                    z = tt(acc[:, :, :], acc[:, :, :], rs[:, :].unsqueeze(1).broadcast_to([128, 4, 256]), ALU.mult, z2, z)
                    yield
                    for j in range(4):
                        a = act(sq[:, j, :], acc[:, j, :], ACT.Silu, z, scale=cw[:, j, 32:33], bias=cw[:, j, 33:34])
                    fl = "p k s -> p (k s)"
                    a = act(mh[:, 0:4, :], sq[:, :, :], ACT.Copy, a)
                    z = tt(ml[:, 0:4, :], sq[:, :, :], mh[:, 0:4, :].bitcast(F32), ALU.subtract, a)
                    parts[4:8] = [(mh[:, k, :], ml[:, k, :], everyrow, z) for k in range(4)]

                def swa():
                    while len(tq) < 4:
                        yield
                    r, tr = head_norm("ev_hn", sbc, qkv[:, :, 0:640], 10, 64, tq)
                    for _ in range(EV_Y):
                        yield
                    v10 = qkv[:, :, 0:640].rearrange("p t (h e) -> p t h e", h=10)
                    z = None
                    for t in range(2):
                        z = tt(v10[:, t], v10[:, t], r[:, t, :].unsqueeze(2).broadcast_to([128, 10, 64]), ALU.mult,
                               tr, z)
                    yield
                    rq = heads_T(qT, 64, 8, lambda h, t: qkv[:, t, h * 64:h * 64 + 64], z, qg[:, 0:1])
                    rk = heads_T(kT, 64, 2, lambda h, t: qkv[:, t, 512 + h * 64:576 + h * 64], z, qg[:, 1:2])
                    yield
                    off = CONSTS["swa"][0]
                    do = yield from attention(
                        "ev_at", sbc, 8, lambda h: qT[:, h, :], lambda h: kT[:, h // 4, :],
                        lambda kt, h: qkv[:, kt, 640 + (h // 4) * 64:704 + (h // 4) * 64],
                        lambda t: cst[:, off + 128 * t:off + 128 * t + 128 * (t + 1)], 0.125, [rq, rk], o, sink=sk)
                    res["o"] = transposed(lambda k, t: o[:, t, k * 128:(k + 1) * 128], 4, mh[:, 4:8, :],
                                          ml[:, 4:8, :], lambda k, t: do[t])

                lo_engine[0] = "pool"
                run(swa(), conv(), products())
                lo_engine[0] = "dve"
                parts[0:4] = [(mh[:, 4 + k, :], ml[:, 4 + k, :], everyrow, res["o"][k // 2]) for k in range(4)]
                r = {}
                run(down_g(parts, 1.0, r), layer_norm())
            return r

        def odd_mixer(gl, tin):
            with ExitStack() as c:
                Q.fence()
                hr, tcol, row = norm_T(gl, tin)
                def sbc(name, shape):
                    return sb(name, shape, c=c)

                u = sb("od_u", [128, 4, 16 + S], c=c)
                w1 = [sb(f"od_w{i}", [128, 3, 16 + S], c=c) for i in range(2)]
                pl = sb("od_pl", [128, 4, S], c=c)
                pw = sb("od_pw", [128, 4, 128], c=c)
                psc = sb("od_psc", [128, 4], c=c)
                qkv = sb("od_qkv", [128, 2, 1536], c=c)
                qT = sb("od_qT", [64, 8, S], c=c)
                kT = sb("od_kT", [64, 8, S], c=c)
                mh = sb("od_mh", [128, 8, S], F32R, c)
                ml = sb("od_ml", [128, 8, S], F32R, c)
                qg = sb("od_qg", [64, 2], c=c)
                zs = [memset(u[:, :, 0:16], 0.0), memset(w1[0][:, :, 0:16], 0.0), memset(w1[1][:, :, 0:16], 0.0)]
                par(pw[:, :, :], A["od_pool_w"][0].rearrange("g c j -> c g j"))
                par(psc[:, :], A["od_pool_scale"][0].rearrange("(g p) -> p g", p=128))
                par(qg[:, 0:1], A["od_q_norm_g"][0].rearrange("(p a) -> p a", a=1))
                tpar = par(qg[:, 1:2], A["od_k_norm_g"][0].rearrange("(p a) -> p a", a=1))
                o = sb("od_o", [128, 2, 512], c=c)
                res = {}
                tq = []
                tv = []
                parts = [None] * 8
                r = {}

                def project(g, to):
                    q0 = yield from x_cols(512, hr)
                    for t in range(2):
                        z = by_token(qkv[:, t, g * 512:(g + 1) * 512], q0[t][1][:, :], t, q0[t][2], tcol)
                        release(q0[t][0], z)
                        to.append(z)

                run(project(0, tq))
                row.diag()
                run(project(1, tq))
                tR = row()

                def pool():
                    yield from project(2, tv)
                    du = []
                    for j0 in (0, 2):
                        i0, wh, wl, sd = take()
                        b, ps, f = bank()
                        w = up_tile(ps, 0, wh, wl, 256, 0, sd, hr, f)
                        yield
                        w = up_tile(ps, 256, wh, wl, 256, 128, sd, hr, f)
                        behind.append((i0, w))
                        a = tt(u[:, j0:j0 + 2, 16:], two(ps[:, :]), R22, ALU.mult, w, tR)
                        release(b, a)
                        du.append(a)
                        yield
                    z = [du, zs]
                    s0 = u
                    lo = 0
                    for step, n in ((1, 4), (2, 3), (4, 2), (8, 1)):
                        g = 4 - n
                        if n == 4:
                            z = tt(pl[:, 0, :], u[:, 0, 16:], u[:, 0, 15:15 + S], ALU.add, z)
                            z = tt(w1[0][:, :, 16:], u[:, 1:4, 16:], u[:, 1:4, 15:15 + S], ALU.add, z)
                            src, k = w1[0], 1
                        else:
                            z = tt(pl[:, g, :], src[:, 3 - n, 16:], src[:, 3 - n, 16 - step:16 - step + S], ALU.add, z)
                            if n > 1:
                                dst = w1[k % 2]
                                z = tt(dst[:, 4 - n:3, 16:], src[:, 4 - n:3, 16:], src[:, 4 - n:3, 16 - step:16 - step + S],
                                       ALU.add, z)
                                src = dst
                                k += 1
                        yield
                    rc = C("rcount").rearrange("p (g s) -> p g s", g=4)
                    z = tt(pl[:, :, 0:16], pl[:, :, 0:16], rc, ALU.mult, z, t_c1)
                    for g in range(4):
                        z = stt(pl[:, g, 16:], pl[:, g, 16:], 1.0 / (2 << g), u[:, g, 32:], ALU.mult, ALU.subtract, z)
                    z = tt(pl[:, :, 0:16], pl[:, :, 0:16], u[:, :, 16:32], ALU.subtract, z)
                    yield
                    for g in range(4):
                        b, ps, f = bank()
                        w = mm(ps[:, 0:256], pw[:, g, :], pl[:, g, :], True, True, f, z, tpar)
                        a = act(mh[:, 4 + g, :], ps[:, 0:256], ACT.Copy, w, tpar, scale=psc[:, g:g + 1])
                        d = stt(ml[:, 4 + g, :], ps[:, 0:256], psc[:, g:g + 1], mh[:, 4 + g, :].bitcast(F32),
                                ALU.mult, ALU.subtract, a)
                        release(b, d)
                    parts[0:4] = [(mh[:, 4 + k, :], ml[:, 4 + k, :], everyrow, d) for k in range(4)]
                    yield
                    yield from down_g(parts, 1.0, r)

                def dil():
                    nr, tr = head_norm("od_hn", sbc, qkv[:, :, 0:1024], 16, 64, tq)
                    for _ in range(OD_Y):
                        yield
                    z = None
                    for t in range(2):
                        v = qkv[:, t, 0:1024].rearrange("p (h e) -> p h e", h=16)
                        z = tt(v, v, nr[:, t, :].unsqueeze(2).broadcast_to([128, 16, 64]), ALU.mult, tr, z)
                    yield
                    rq = heads_T(qT, 64, 8, lambda h, t: qkv[:, t, h * 64:h * 64 + 64], [z, tpar], qg[:, 0:1])
                    yield
                    rk = heads_T(kT, 64, 8, lambda h, t: qkv[:, t, 512 + h * 64:576 + h * 64], [z, tpar], qg[:, 1:2])
                    yield
                    off, of2 = CONSTS["dil"][0], CONSTS["mult"][0]
                    do = yield from attention(
                        "od_at", sbc, 8, lambda h: qT[:, h, :], lambda h: kT[:, h, :],
                        lambda kt, h: qkv[:, kt, 1024 + h * 64:1088 + h * 64],
                        lambda t: cst[:, off + 128 * t:off + 128 * t + 128 * (t + 1)], 0.125, [rq, rk, tv], o,
                        mult=lambda t: cst[:, of2 + 128 * t:of2 + 128 * t + 128 * (t + 1)])
                    yield
                    to = transposed(lambda k, t: o[:, t, k * 128:(k + 1) * 128], 4, mh[:, 0:4, :],
                                    ml[:, 0:4, :], lambda k, t: do[t])
                    parts[4:8] = [(mh[:, k, :], ml[:, k, :], everyrow, to[k // 2]) for k in range(4)]

                run(dil(), pool())
            return r

        def rope_tables(cs, sn, c, done):
            pi_ = sb("rp_i", [128, 2], I32, c)
            pf = sb("rp_f", [128, 2], c=c)
            w = [sb(f"rp_w{i}", [128, 2, 16], c=c) for i in range(4)]
            tpar = par(pi_[:, :], A["positions_2"][0].rearrange("(t p) -> p t", p=128))
            yield
            z = cp(pf[:, :], pi_[:, :], tpar)
            for t in range(2):
                z = ts(w[0][:, t, :], C("invf"), pf[:, t:t + 1], None, ALU.mult, None, z, t_c)
            magic = 12582912.0
            z = ts(w[1][:, :, :], w[0][:, :, :], 1.0 / (2 * np.pi), magic, ALU.mult, ALU.add, z)
            z = ts(w[1][:, :, :], w[1][:, :, :], -magic, None, ALU.add, None, z)
            yield
            c1 = 6.28125
            c2 = float(np.float32(np.round((2 * np.pi - c1) * 2 ** 20) / 2 ** 20))
            c3 = float(2 * np.pi - c1 - c2)
            for k in (c1, c2, c3):
                z = stt(w[0][:, :, :], w[1][:, :, :], -k, w[0][:, :, :], ALU.mult, ALU.add, z)
            top = 3.1415925
            z = ts(w[0][:, :, :], w[0][:, :, :], top, -top, ALU.min, ALU.max, z)
            yield
            a = act(sn, w[0][:, :, :], ACT.Sin, z)
            z = ts(w[2][:, :, :], w[0][:, :, :], -1.0, None, ALU.mult, None, z)
            z = tt(w[2][:, :, :], w[2][:, :, :], w[0][:, :, :], ALU.max, z)
            z = ts(w[3][:, :, :], w[2][:, :, :], -1.0, float(np.pi / 2), ALU.mult, ALU.add, z)
            done.append(act(cs, w[3][:, :, :], ACT.Sin, z, a))

        def mixer2(l, gl, tin, csn, t_rope):
            P = f"m{l}_"
            with ExitStack() as c:
                Q.fence()
                hr, tcol, row = norm_T(gl, tin)
                W0 = 416
                nat = sb(P + "nat", [128, 2, 1880], c=c)
                G = sb(P + "G", [128, 32, S], c=c)
                bh = sb(P + "bh", [128, 8, S], F32R, c)
                bl = sb(P + "bl", [128, 8, S], F32R, c)
                cvw = sb(P + "cvw", [128, 2, 3], c=c)
                gup = sb(P + "gup", [16, 128], c=c)
                gbg = sb(P + "gbg", [128, 1], c=c)
                gng = sb(P + "gng", [128, 64], c=c)
                qng = sb(P + "qng", [128, 2], c=c)
                kng = sb(P + "kng", [128, 1], c=c)
                SCR = 12320
                scr = sb(P + "scr", [128, SCR], c=c)
                R_DSA, R_GLA = (0, 6240), (6240, SCR)
                if l == 0:
                    Q.dma("sp", cst[:, KEEP:KEEP + SECOND], A["consts"][:, FIRST:FIRST + SECOND], s_c, 32, t_c1, Q.past)
                tc2 = (s_c, 32)
                for t in range(2):
                    par(cvw[:, t, :], A["conv_w_2"][l][:, t * 128:(t + 1) * 128].rearrange("k p -> p k"))
                par(gup[:, :], A["gla_w_gate_up_2"][l])
                par(gbg[:, :], A["gla_b_gate_2"][l].rearrange("(p a) -> p a", a=1))
                par(gng[:, :], A["gla_norm_g_2"][l].rearrange("(a n) -> a n", a=1).broadcast_to([128, 64]))
                par(qng[:, :], A["mla_q_norm_g_2"][l].rearrange("(k p) -> p k", p=128))
                tpar = par(kng[:, :], A["mla_kv_norm_g_2"][l].rearrange("(p a) -> p a", a=1))

                tn = {}

                def project(groups):
                    for c0, n, at in groups:
                        q0 = yield from x_cols(n, hr)
                        for t in range(2):
                            z = by_token(nat[:, t, at:at + n], q0[t][1][:, 0:n], t, q0[t][2], tcol,
                                         e="act" if t else "dve")
                            release(q0[t][0], z)
                            tn[at, t] = z

                run(project(X2[0:1]))
                row.diag()
                run(project(X2[1:2]))
                tR = row()
                tnat = [tn[at, t] for c0, n, at in X2[0:2] for t in range(2)]

                def N(a, b, t=None):
                    return nat[:, :, W0 + a:W0 + b] if t is None else nat[:, t, W0 + a:W0 + b]

                res = {}
                parts = []

                bks = []

                def short_conv():
                    cT, y = G[:, 0:2, :], G[:, 2:4, :]
                    uu = G[:, 4:8, :].rearrange("p a s -> p (a s)")[:, 0:2 * (2 + S)]\
                        .rearrange("p (a s) -> p a s", a=2)
                    z0 = memset(uu[:, :, 0:2], 0.0)
                    while len(bks) < 3:
                        yield
                    z = tt(cT[:, :, :], bks[1][1], R22, ALU.mult, bks[1][2], tR)
                    release(bks[1][0], z)
                    z = tt(cT[:, :, :], cT[:, :, :], R22, ALU.mult, z)
                    z = tt(uu[:, :, 2:], bks[2][1], cT[:, :, :], ALU.mult, bks[2][2], z)
                    release(bks[2][0], z)
                    yield
                    for j in range(2):
                        z = ts(y[:, j, :], uu[:, j, 0:S], cvw[:, j, 0:1], None, ALU.mult, None, z, z0, tpar)
                        for k in (1, 2):
                            z = stt(y[:, j, :], uu[:, j, k:k + S], cvw[:, j, k:k + 1], y[:, j, :], ALU.mult,
                                    ALU.add, z)
                    yield
                    z = tt(y[:, :, :], y[:, :, :], bks[0][1], ALU.mult, z, bks[0][2])
                    release(bks[0][0], z)
                    z = tt(y[:, :, :], y[:, :, :], R22, ALU.mult, z)
                    a = act(bh[:, 2:4, :], y[:, :, :], ACT.Copy, z)
                    res[1] = tt(bl[:, 2:4, :], y[:, :, :], bh[:, 2:4, :].bitcast(F32), ALU.subtract, a)

                def gates():
                    yield from project(X2[2:4])
                    for g in range(3):
                        i0, wh, wl, sd = take()
                        b, ps, f = bank()
                        w = up_tile(ps, 0, wh, wl, 256, 0, sd, hr, f)
                        yield
                        w = up_tile(ps, 256, wh, wl, 256, 128, sd, hr, f)
                        behind.append((i0, w))
                        bks.append((b, two(ps[:, :]), w))
                        yield
                    tg = {}
                    halves = []

                    def low(q4, src, hh, a):
                        z = stt(hTl[:, 2 * q4:2 * q4 + 2, :], src, 0.5, hh.bitcast(F32), ALU.mult, ALU.subtract, a)
                        parts.extend((hTh[:, 2 * q4 + j, :], hTl[:, 2 * q4 + j, :], everyrow, z) for j in range(2))

                    for n, merge in FILL:
                        if not merge:
                            for g in range(4 * n, 4 * n + 4):
                                i0, wh, wl, sd = take()
                                b, ps, f = bank()
                                w = up_tile(ps, 0, wh, wl, 256, 0, sd, hr, f)
                                yield
                                w = up_tile(ps, 256, wh, wl, 256, 128, sd, hr, f)
                                behind.append((i0, w))
                                gg = G[:, 2 * g:2 * g + 2, :]
                                z = tt(gg, two(ps[:, :]), R22, ALU.mult, w, None if n else res[1], tR)
                                release(b, z)
                                tg[g] = act(gg, gg, ACT.Tanh, z, scale=0.5)
                                yield
                            hfree = w
                            continue
                        while n not in res:
                            yield
                        i0, wh, wl, sd = take()
                        for q4 in range(4):
                            b, ps, f = bank()
                            for j in range(2):
                                fcol = (2 * q4 + j) * 128
                                for kk in range(2):
                                    w = mm3(ps[:, 256 * j:256 * j + 256],
                                            wh[:, kk * 1024 + fcol:kk * 1024 + fcol + 128],
                                            wl[:, kk * 1024 + fcol:kk * 1024 + fcol + 128], bh[:, 2 * n + kk, :],
                                            bl[:, 2 * n + kk, :], kk == 0, kk == 1, f, sd, res[n], sig=(kk == 1))
                            g = G[:, 8 * n + 2 * q4:8 * n + 2 * q4 + 2, :]
                            z = stt(g, g, 1.0, two(ps[:, :]), ALU.add, ALU.mult, w, tg[4 * n + q4])
                            release(b, z)
                            if n != 1:
                                o_ = G[:, 8 + 2 * q4:8 + 2 * q4 + 2, :]
                                z = tt(o_, o_, g, ALU.add, z, res["acc", q4], e="pool" if n and q4 != 3 else "dve")
                            res["acc", q4] = z
                            if q4 == 3:
                                lo_engine[0] = "dve" if n == 0 else "pool"
                                used(i0, w)
                            if n == 0:
                                hh = hTh[:, 2 * q4:2 * q4 + 2, :]
                                halves.append((q4, o_, hh, act(hh, o_, ACT.Copy, z, hfree, scale=0.5)))
                                if q4:
                                    low(*halves.pop(0))
                            yield
                    low(*halves.pop(0))

                def finish(n, o, do):
                    res[n] = transposed(lambda k, t: o[:, t, k * 128:(k + 1) * 128], 2, bh[:, 2 * n:2 * n + 2, :],
                                        bl[:, 2 * n:2 * n + 2, :], lambda k, t: do[t])

                def causal(t):
                    off = CONSTS["causal"][0]
                    return cst[:, off + 128 * t:off + 128 * t + 128 * (t + 1)]

                def mla():
                    cc = Region(scr, 0, SCR)
                    wq = cc(P + "wq", [128, 2, 384])
                    wkv = cc(P + "wkv", [128, 512])
                    par(wq, A["mla_w_q_up_2"][l].rearrange("(k p) n -> p k n", p=128))
                    tpw = par(wkv, A["mla_w_kv_up_2"][l])
                    cqT = cc(P + "cqT", [128, 3, S])
                    qn = cc(P + "qn", [128, 2, 384])
                    kn = cc(P + "kn", [128, 2, 384])
                    vn = cc(P + "vn", [128, 2, 256])
                    qT = cc(P + "qT", [96, 4, S])
                    kT = cc(P + "kT", [96, 4, S])
                    rw = [cc(P + f"rw{i}", [128, 2, 64]) for i in range(4)]
                    r, tr = head_norm(P + "cq", cc, nat[:, :, 0:256], 1, 256, tnat)
                    r2, tr2 = head_norm(P + "ck", cc, nat[:, :, 256:384], 1, 128, tnat)
                    yield
                    z = None
                    for t in range(2):
                        z = ts(nat[:, t, 0:256], nat[:, t, 0:256], r[:, t, 0:1], None, ALU.mult, None, tr, z)
                        z = ts(nat[:, t, 256:384], nat[:, t, 256:384], r2[:, t, 0:1], None, ALU.mult, None, tr2, z)
                    yield
                    yield
                    b, ps, f = bank()
                    b2, ps2, f2 = bank()
                    for k in range(3):
                        for t in range(2):
                            o = (ps if k < 2 else ps2)[:, (2 * (k % 2) + t) * 128:(2 * (k % 2) + t) * 128 + 128]
                            w = tp(o, nat[:, t, k * 128:k * 128 + 128], ident, f, f2, z)
                    for k in range(3):
                        g = qng[:, k:k + 1] if k < 2 else kng[:, 0:1]
                        p_ = (ps if k < 2 else ps2)[:, 256 * (k % 2):256 * (k % 2) + 256]
                        a = act(cqT[:, k, :], p_, ACT.Copy, w, tpar, scale=g)
                    release(b, a)
                    release(b2, a)
                    yield
                    zz = []
                    for t in range(2):
                        sl = slice(t * 128, t * 128 + 128)
                        b, ps, f = bank()
                        for k in range(2):
                            w = mm(ps[:, 0:384], cqT[:, k, sl], wq[:, k, :], k == 0, k == 1, f, a, tpw)
                        z = cp(qn[:, t, :], ps[:, 0:384], w, e="act")
                        release(b, z)
                        b, ps, f = bank()
                        w = mm(ps[:, :], cqT[:, 2, sl], wkv[:, :], True, True, f, a)
                        pv = ps[:, :].rearrange("p (h e) -> p h e", h=4)
                        z1 = cp(kn[:, t, :].rearrange("p (h e) -> p h e", h=4)[:, :, 0:64], pv[:, :, 0:64], w)
                        z2 = cp(vn[:, t, :].rearrange("p (h e) -> p h e", h=4), pv[:, :, 64:128], z1)
                        release(b, z2)
                        zz += [z, z1, z2]
                    yield
                    z = [zz, t_rope]
                    cs, sn = csn

                    def b4(x):
                        return x.unsqueeze(1).broadcast_to([128, 4, 16])

                    for t in range(2):
                        q4 = qn[:, t, :].rearrange("p (h e) -> p h e", h=4)
                        x1, x2 = q4[:, :, 64:80], q4[:, :, 80:96]
                        v = [rw[i][:, t, :].rearrange("p (h e) -> p h e", h=4) for i in range(4)]
                        ct, st = b4(cs[:, t, :]), b4(sn[:, t, :])
                        za = tt(v[0], x1, ct, ALU.mult, z)
                        zb = tt(v[1], x2, st, ALU.mult, z)
                        zc = tt(v[2], x1, st, ALU.mult, z)
                        zd = tt(v[3], x2, ct, ALU.mult, z)
                        z1 = tt(x1, v[0], v[1], ALU.subtract, zd)
                        zq = tt(x2, v[2], v[3], ALU.add, z1)
                        kr = nat[:, t, 384:416]
                        k1, k2 = kr[:, 0:16], kr[:, 16:32]
                        c_, s_ = cs[:, t, :], sn[:, t, :]
                        m = [rw[i][:, t, 0:16] for i in range(4)]
                        za = tt(m[0], k1, c_, ALU.mult, zq)
                        zb = tt(m[1], k2, s_, ALU.mult, zq)
                        zc = tt(m[2], k1, s_, ALU.mult, zq)
                        zd = tt(m[3], k2, c_, ALU.mult, zq)
                        k4 = kn[:, t, :].rearrange("p (h e) -> p h e", h=4)
                        z1 = tt(k4[:, :, 64:80], b4(m[0]), b4(m[1]), ALU.subtract, zd)
                        zk = tt(k4[:, :, 80:96], b4(m[2]), b4(m[3]), ALU.add, z1)
                        z = [zk]
                        yield
                    rq = heads_T(qT, 96, 4, lambda h, t: qn[:, t, h * 96:h * 96 + 96], z)
                    yield
                    rk = heads_T(kT, 96, 4, lambda h, t: kn[:, t, h * 96:h * 96 + 96], z)
                    yield
                    o = nat[:, :, 0:256]
                    do = yield from attention(
                        P + "mat", cc, 4, lambda h: qT[:, h, :], lambda h: kT[:, h, :],
                        lambda kt, h: vn[:, kt, h * 64:h * 64 + 64], causal, 96 ** -0.5, [rq, rk, tc2], o)
                    yield
                    finish(0, o, do)

                def dsa():
                    cc = Region(scr, *R_DSA)
                    iqT = cc(P + "iqT", [128, 2, S])
                    ikT = cc(P + "ikT", [128, 1, S])
                    ik4 = cc(P + "ik4", [128, 2, 128])
                    rl = [cc(P + f"rl{i}", [128, 512]) for i in range(2)]
                    sc = cc(P + "sc", [128, 384])
                    iw = cc(P + "iw", [128, 2, 8])
                    m8 = cc(P + "m8", [128, 8])
                    qT = cc(P + "dqT", [128, 2, S])
                    kT = cc(P + "dkT", [128, 1, S])
                    dk2 = cc(P + "dk2", [128, 2, 128])
                    z1, z2 = [], []
                    for t in range(2):
                        z1.append(cp(ik4[:, t, :].rearrange("p (a e) -> p a e", a=4),
                                     N(640, 672, t).unsqueeze(1).broadcast_to([128, 4, 32]), tnat))
                        z2.append(cp(dk2[:, t, :].rearrange("p (a e) -> p a e", a=2),
                                     N(256, 320, t).unsqueeze(1).broadcast_to([128, 2, 64]), tnat))
                    ri = heads_T(iqT, 128, 2, lambda h, t: N(384 + h * 128, 512 + h * 128, t), tnat)
                    yield
                    rk = heads_T(ikT, 128, 1, lambda h, t: ik4[:, t, :], z1)
                    ti = ts(iw[:, :, :], N(672, 680), 8.0 ** -0.5, None, ALU.mult, None, tnat)
                    yield
                    rq = heads_T(qT, 128, 2, lambda h, t: N(h * 128, h * 128 + 128, t), tnat)
                    rkk = heads_T(kT, 128, 1, lambda h, t: dk2[:, t, :], z2)
                    yield
                    rf = [None, None]
                    masks = []
                    for t in range(2):
                        nk = 128 * (t + 1)
                        s_ = sc[:, 128 * t:128 * t + nk]
                        z = ti
                        for h0 in range(4):
                            i = h0 % 2
                            b, ps, f = bank()
                            rows = slice(32 * h0, 32 * h0 + 32)
                            for j in range(2):
                                w = mm(ps[:, j * nk:(j + 1) * nk], iqT[rows, j, t * 128:t * 128 + 128],
                                       ikT[rows, 0, 0:nk], True, True, f, ri, rk)
                            a = act(rl[i][:, 0:2 * nk], ps[:, 0:2 * nk], ACT.Relu, w, rf[i], scale=32.0 ** -0.5)
                            release(b, a)
                            for j in range(2):
                                h = h0 + 4 * j
                                z = stt(s_, rl[i][:, j * nk:(j + 1) * nk], iw[:, t, h:h + 1],
                                        causal(t) if h == 0 else s_, ALU.mult, ALU.add, a, z, tc2)
                            rf[i] = z
                            yield
                        for r_ in range(8):
                            z = op("dve", lambda g, s_=s_: g.max(m8[:, :], s_), z)
                            z = op("dve", lambda g, s_=s_: g.match_replace(s_, m8[:, :], s_, TAKEN), z)
                            if r_ % 2:
                                yield
                        z = ts(s_, s_, -2e38, NEG, ALU.is_gt, ALU.mult, z)
                        z = tt(s_, s_, causal(t), ALU.add, z)
                        masks.append(z)
                        yield
                    o = N(0, 256)
                    do = yield from attention(
                        P + "dat", cc, 4, lambda h: qT[64 * (h % 2):64 * (h % 2) + 64, h // 2, :],
                        lambda h: kT[64 * (h % 2):64 * (h % 2) + 64, 0, :],
                        lambda kt, h: N(320, 384, kt), lambda t: sc[:, 128 * t:128 * t + 128 * (t + 1)],
                        0.125, [rq, rkk], o, mready=masks, apart=True)
                    yield
                    finish(2, o, do)

                def gla():
                    cc = Region(scr, *R_GLA)
                    B = {}

                    def buf(n, shape=(128, S)):
                        B[n] = cc(P + "g_" + n, list(shape))
                        return B[n]

                    qT, kT, cum, e1, e2 = (buf(n) for n in ("q", "k", "cum", "e1", "e2"))
                    glT = buf("gl", (16, S))
                    qz = buf("qz", (128, 4, 128))
                    kq = buf("kq", (128, 4, S))
                    kl, ql = [kq[:, 0, :], kq[:, 1, :]], [kq[:, 2, :], kq[:, 3, :]]
                    at = buf("at", (128, 2, 4, 128))
                    kd = buf("kd", (128, 2, 128))
                    st = buf("st", (128, 3, 256))
                    um = buf("um", (128, 256))
                    o = buf("o", (128, 2, 256))
                    og = kq[:, 2:4, :]
                    el = buf("el", (128, 4))
                    z0 = memset(qz[:, :, :], 0.0)
                    z1 = memset(at[:, :, :, :], 0.0)
                    b, ps, f = bank()
                    for j, a0 in enumerate((680, 808)):
                        for t in range(2):
                            w = tp(ps[:, (2 * j + t) * 128:(2 * j + t) * 128 + 128], N(a0, a0 + 128, t), ident, f,
                                   tnat)
                    tq = act(qT[:, :], ps[:, 0:256], ACT.Copy, w, scale=32.0 ** -0.5)
                    tk = act(kT[:, :], ps[:, 256:512], ACT.Copy, w)
                    release(b, tk)
                    b, ps, f = bank()
                    for t in range(2):
                        w = tp(ps[0:16, t * 128:t * 128 + 128], N(1192, 1208, t), ident, f, tnat)
                    a = cp(glT[:, :], ps[0:16, 0:256], w)
                    release(b, a)
                    yield
                    b, ps, f = bank()
                    w = mm(ps[:, 0:256], gup[:, :], glT[:, :], True, True, f, a, tpar)
                    z = ts(cum[:, :], ps[:, 0:256], gbg[:, 0:1], None, ALU.add, None, w, tpar)
                    release(b, z)
                    zz = z
                    z = ts(e1[:, :], cum[:, :], -1.0, None, ALU.mult, None, z)
                    z = tt(e1[:, :], e1[:, :], cum[:, :], ALU.max, z)
                    a = act(e1[:, :], e1[:, :], ACT.Exp, z, scale=-1.0)
                    a = act(e1[:, :], e1[:, :], ACT.Ln, a, bias=1.0)
                    z = ts(cum[:, :], cum[:, :], 0.0, None, ALU.min, None, a)
                    z = tt(e1[:, :], cum[:, :], e1[:, :], ALU.subtract, z)
                    z = ts(e1[:, :], e1[:, :], 1.0 / 16, None, ALU.mult, None, z)
                    yield
                    zc = memset(e2[:, :], 0.0, z, e="dve")
                    for cch in range(4):
                        sl = slice(cch * 64, cch * 64 + 64)
                        z = op("dve", lambda g, sl=sl: g.tensor_tensor_scan(cum[:, sl], e1[:, sl], e2[:, sl], 0.0,
                                                                           ALU.add, ALU.add), zc)
                    tc = z
                    yield
                    yield
                    a = act(e1[:, :], cum[:, :], ACT.Exp, tc)
                    cq = cum[:, :].rearrange("p (c s) -> p c s", c=4)
                    for cch in range(4):
                        o0 = 64 * (cch % 2)
                        z = tt(qz[:, cch, o0:o0 + 64], qT[:, cch * 64:cch * 64 + 64], e1[:, cch * 64:cch * 64 + 64],
                               ALU.mult, a, tq, z0)
                    z = cp(el[:, :], e1[:, :].rearrange("p (c s) -> p c s", c=4)[:, :, 63], z)
                    tqz = z
                    yield
                    z = tt(e2[:, :].rearrange("p (c s) -> p c s", c=4), cq[:, :, 63:64].broadcast_to([128, 4, 64]),
                           cq, ALU.subtract, z)
                    a = act(e2[:, :], e2[:, :], ACT.Exp, z)
                    z = tt(e2[:, :], e2[:, :], kT[:, :], ALU.mult, a, tk)
                    yield
                    b, ps, f = bank()
                    for t in range(2):
                        w = tp(ps[:, t * 128:t * 128 + 128], e2[:, t * 128:t * 128 + 128], ident, f, z)
                    tkd = cp(kd[:, :, :].rearrange("p a b -> p (a b)"), ps[:, 0:256], w)
                    release(b, tkd)
                    yield
                    tst = []
                    zprev = None
                    for cch in range(3):
                        t, p0 = cch // 2, 64 * (cch % 2)
                        b, ps, f = bank()
                        w = mm(ps[:, 0:256], kd[p0:p0 + 64, t, :], N(936, 1192, t)[p0:p0 + 64, :], True, True, f,
                               tkd, tnat)
                        if cch == 0:
                            z = tt(st[:, 0, :], ps[:, 0:256], C("block"), ALU.mult, w, tc2)
                            release(b, z)
                        else:
                            z = tt(um[:, :], ps[:, 0:256], C("block"), ALU.mult, w, zprev)
                            release(b, z)
                            z = stt(st[:, cch, :], st[:, cch - 1, :], el[:, cch:cch + 1], um[:, :], ALU.mult,
                                    ALU.add, z, zprev, tqz)
                        zprev = z
                        tst.append(z)
                        yield
                    mm_done = {-1: None, 0: None}
                    ready = {0: (qT, kT, [tq, tk])}
                    tat = z1

                    def decays(lev):
                        s_ = 1 << (lev - 1)
                        n2 = S // (2 * s_)
                        cv = cum[:, :].rearrange("p (n s) -> p n s", s=2 * s_)
                        ev_ = e1[:, :].rearrange("p (n s) -> p n s", s=2 * s_)
                        refb = cv[:, :, s_ - 1:s_].broadcast_to([128, n2, s_])
                        za = tt(ev_[:, :, 0:s_], refb, cv[:, :, 0:s_], ALU.subtract, tc, tqz, ready[lev - 1][2])
                        zb = tt(ev_[:, :, s_:], cv[:, :, s_:], refb, ALU.subtract, za)
                        return act(e1[:, :], e1[:, :], ACT.Exp, zb)

                    def scaled(lev, a):
                        qq, kk = ql[lev % 2], kl[lev % 2]
                        zk = tt(kk[:, :], kT[:, :], e1[:, :], ALU.mult, a, tk, mm_done[lev - 2], e="pool")
                        zq = tt(qq[:, :], qT[:, :], e1[:, :], ALU.mult, a, tq, mm_done[lev - 2])
                        ready[lev] = (qq, kk, [zq, zk])

                    for lev in range(7):
                        if lev < 6:
                            a = decays(lev + 1)
                        yield
                        qq, kk, zl = ready[lev]
                        if lev < 6:
                            scaled(lev + 1, a)
                        bs = [bank(), bank()]
                        ws = [None, None]
                        for h in range(4):
                            for t in range(2):
                                sl = slice(t * 128, t * 128 + 128)
                                ws[t] = mm(bs[t][1][:, h * 128:h * 128 + 128], kk[32 * h:32 * h + 32, sl],
                                           qq[32 * h:32 * h + 32, sl], True, True, bs[t][2], zl, ws[t])
                        lm = C("levels", 128 * lev, 128).bitcast(I32).unsqueeze(1).broadcast_to([128, 4, 128])
                        for t in range(2):
                            tat = op("dve", lambda g, o_=at[:, t, :, :], lm=lm,
                                     d_=bs[t][1][:, :].rearrange("p (a s) -> p a s", a=4):
                                     g.copy_predicated(o_, lm, d_), ws[t], tat, tc2)
                            release(bs[t][0], tat)
                        w = ws
                        mm_done[lev] = w
                        yield
                    do = []
                    for t in range(2):
                        b, ps, f = bank()
                        first = True
                        for cch in (2 * t, 2 * t + 1):
                            if cch == 0:
                                continue
                            w = mm(ps[:, 0:256], qz[:, cch, :], st[:, cch - 1, :], first, False, f, tqz,
                                   tst[cch - 1], sig=False)
                            first = False
                        for h in range(4):
                            w = mm(ps[:, h * 64:h * 64 + 64], at[:, t, h, :], N(936 + h * 64, 1000 + h * 64, t),
                                   False, h == 3, tat, sig=(h == 3))
                        z = cp(o[:, t, :], ps[:, 0:256], w, e="act")
                        release(b, z)
                        do.append(z)
                    yield
                    r, tr = head_norm(P + "gn", cc, o[:, :, :], 4, 64, do, sq=kq[:, 0:2, :])
                    yield
                    grv = N(1208, 1464)
                    a = act(og[:, :, :], grv, ACT.Tanh, tnat, do, scale=0.5)
                    z = stt(og[:, :, :], og[:, :, :], 1.0, grv, ALU.add, ALU.mult, a)
                    z = ts(og[:, :, :], og[:, :, :], 0.5, None, ALU.mult, None, z)
                    yield
                    for t in range(2):
                        ov = o[:, t, :].rearrange("p (h e) -> p h e", h=4)
                        z = tt(ov, ov, r[:, t, :].unsqueeze(2).broadcast_to([128, 4, 64]), ALU.mult, tr, z)
                        z = tt(ov, ov, gng[:, :].unsqueeze(1).broadcast_to([128, 4, 64]), ALU.mult, z, tpar)
                    yield
                    z = tt(o[:, :, :], o[:, :, :], og[:, :, :], ALU.mult, z)
                    yield
                    yield
                    finish(3, o, [z, z])

                def chains():
                    one, two_ = dsa(), gla()
                    waiting = [one]
                    while waiting or two_ is not None:
                        if two_ is not None and (X2[2][2], 1) in tn and two_ not in waiting:
                            tg = [tn[X2[2][2], t] for t in range(2)]
                            tnat.extend(tg)
                            waiting.append(two_)
                        for g in list(waiting):
                            if next(g, "end") == "end":
                                waiting.remove(g)
                                if g is two_:
                                    two_ = None
                        yield
                    while (0, 1) not in tn:
                        yield
                    tnat.extend(tn[0, t] for t in range(2))
                    Q.fence([res[2], res[3]])
                    yield from mla()

                lo_engine[0] = "pool"
                run(gates(), short_conv(), chains())
                lo_engine[0] = "dve"
                r = down(parts, 1.0)
            return r

        issue_split()
        behind.extend([None] * (NH - 1))
        b, ps, f = bank()
        for k in range(8):
            w = tp(ps[:, 16 * k:16 * k + 10], grow[:, k * 128:k * 128 + 128], ident[0:10, 0:10], f, t_g, t_c)
        t_gc = cp(gcol[:, :, 0:10], ps[:, 0:128].rearrange("p (k g) -> p k g", k=8)[:, :, 0:10], w, e="act")
        release(b, t_gc)

        cs, sn = rope[:, 0], rope[:, 1]
        t_rope = []
        later.append(rope_tables(cs, sn, cr, t_rope))
        next(later[0])
        fin = stage[0][:, :].rearrange("p (t d) -> p t d", t=2)
        t = t_x
        stages = [lambda t: ffn(0, 0, t, 0.5), lambda t: even_mixer(1, t), lambda t: ffn(1, 2, t, 0.5),
                  lambda t: ffn(2, 3, t, 0.5), lambda t: odd_mixer(4, t), lambda t: ffn(3, 5, t, 0.5)]
        for l in range(2):
            stages += [lambda t, l=l: mixer2(l, 6 + l, t, (cs, sn), t_rope),
                       lambda t, l=l: ffn(4 + l, 8 + l, t, 1.0)]
        for s in stages:
            if s is not stages[0]:
                flush()
                cr.close()
            t = s(t)
        gfin = stage[1][:, 0:D]
        t_gf = par(gfin, A["final_norm_g_2"].rearrange("(a n) -> a n", a=1).broadcast_to([128, D]), stage_free)
        tcol = rms_col(t)
        for h in range(2):
            z = stt(fin[:, h, :], xs[:, h, :], st8[:, 4 + h:5 + h], gfin, ALU.mult, ALU.mult, tcol, t_gf)
            Q.dma("act", out[0].rearrange("(t p) d -> p t d", p=128)[:, h, :], fin[:, h, :], s_o, 16 * (h + 1), z)
        Q.waits("act", [(s_o, 32)])
        block = ctx.enter_context(nc.Block())
        Q.emit(block)


def kernel(**inputs):
    import numpy as _np
    import concourse.bacc as _bacc
    from concourse import mybir as _mybir
    from concourse.bass_utils import run_bass_kernel_spmd as _run

    nc = _bacc.Bacc("TRN2", target_bir_lowering=False, num_devices=1)
    arrays, A = {}, {}
    given = dict(inputs)
    given["consts"] = CONST_ARRAY
    for name, a in given.items():
        a = _np.ascontiguousarray(a)
        arrays[f"in_{name}"] = a
        A[name] = nc.dram_tensor(f"in_{name}", a.shape, _mybir.dt.from_np(a.dtype), kind="ExternalInput").ap()
    out = nc.dram_tensor("out_0", (1, S, D), F32, kind="ExternalOutput").ap()
    build(nc, A, out)
    r = _run(nc, [arrays], core_ids=[0])
    return r.results[0]["out_0"]
```
